# Optimizing a Trainium2 kernel written in Bass

```python
import math
import jax, jax.numpy as jnp
from jax import lax
import numpy as np
import jax
import jax.numpy as jnp

D_MODEL = 1024
BATCH = 1
SEQ = 256
DEPTH = 2

D_CONV = D_MODEL
CONV_GROUPS = 8
SHORT_CONV_K = 3
D_RNN = D_MODEL
RNN_HEADS = 4
RNN_HEAD_DIM = D_RNN // RNN_HEADS
RNN_CONV_K = 4
LRU_C = 8.0
N_BRANCH = 2
D_FF = 2816
D_IN = 3 * D_CONV + 2 * D_RNN + N_BRANCH * D_MODEL
SPLITS = (D_CONV, 2 * D_CONV, 3 * D_CONV, 3 * D_CONV + D_RNN, 3 * D_CONV + 2 * D_RNN)
ALPHA = (2.0 * DEPTH) ** 0.25
BETA = (8.0 * DEPTH) ** -0.25
LN_EPS = 1e-5


def layer_norm(x, g, b):
    xf = x.astype(jnp.float32)
    mu = jnp.mean(xf, axis=-1, keepdims=True)
    var = jnp.mean(jnp.square(xf - mu), axis=-1, keepdims=True)
    y = (xf - mu) * lax.rsqrt(var + LN_EPS)
    return (y * g.astype(jnp.float32) + b.astype(jnp.float32)).astype(x.dtype)

def causal_depthwise_conv(x, w, k):
    s = x.shape[1]
    xp = jnp.pad(x, ((0, 0), (k - 1, 0), (0, 0)))
    out = xp[:, 0:s, :] * w[0]
    for i in range(1, k):
        out = out + xp[:, i:i + s, :] * w[i]
    return out

def swiglu(x, w1, w2):
    g, u = jnp.split(x @ w1, 2, axis=-1)
    return (jax.nn.silu(g) * u) @ w2

def rg_lru(x, gate_in, gate_rec, a_param):
    s = x.shape[1]
    log_a = -LRU_C * gate_rec * jax.nn.softplus(-a_param)
    a = jnp.exp(log_a)
    mult = jnp.sqrt(-jnp.expm1(2.0 * log_a))
    is_start = (jnp.arange(s) == 0)[None, :, None]
    mult = jnp.where(is_start, 1.0, mult)
    b = x * gate_in * mult

    def combine(left, right):
        a1, b1 = left
        a2, b2 = right
        return a1 * a2, a2 * b1 + b2

    _, h = lax.associative_scan(combine, (a, b), axis=1)
    return h

def hybrid_mixer(x, w_in, b_merge, sc_w, rc_w, rc_b, rg_w, rg_b, a_param,
                 w_out_conv, w_out_rnn, w_o):
    bsz, s, _ = x.shape
    proj = x @ w_in
    b_gate, c_gate, v, x_r, y_r, g_logits = jnp.split(proj, SPLITS, axis=-1)

    y_a = (b_gate * causal_depthwise_conv(c_gate * v, sc_w, SHORT_CONV_K)) @ w_out_conv

    xc = causal_depthwise_conv(x_r, rc_w, RNN_CONV_K) + rc_b
    xh = xc.reshape(bsz, s, RNN_HEADS, RNN_HEAD_DIM)
    gates = jnp.einsum('bshi,ghij->gbshj', xh, rg_w).reshape(2, bsz, s, D_RNN)
    gates = jax.nn.sigmoid((gates + rg_b[:, None, None, :]).astype(jnp.float32))
    h = rg_lru(xc.astype(jnp.float32), gates[0], gates[1],
               a_param.astype(jnp.float32)).astype(x.dtype)
    y_b = (h * jax.nn.gelu(y_r)) @ w_out_rnn

    g_a, g_b = jnp.split(jax.nn.sigmoid(g_logits + b_merge), 2, axis=-1)
    return (g_a * y_a + g_b * y_b) @ w_o

def first_inputs(seed: int = 0) -> dict:
    key = jax.random.key(seed)
    ks = jax.random.split(key, 20)
    f32 = jnp.float32
    nrm = lambda k, shape, scale: jax.random.normal(k, shape, f32) * scale

    x = jax.random.normal(ks[0], (BATCH, SEQ, D_MODEL), f32)
    w_in = nrm(ks[1], (DEPTH, D_MODEL, D_IN), D_MODEL ** -0.5)
    b_merge = nrm(ks[2], (DEPTH, N_BRANCH * D_MODEL), 0.1)
    sc_w = nrm(ks[3], (DEPTH, SHORT_CONV_K, D_CONV), SHORT_CONV_K ** -0.5)
    rc_w = nrm(ks[4], (DEPTH, RNN_CONV_K, D_RNN), RNN_CONV_K ** -0.5)
    rc_b = nrm(ks[5], (DEPTH, D_RNN), 0.02)
    rg_w = nrm(ks[6], (DEPTH, 2, RNN_HEADS, RNN_HEAD_DIM, RNN_HEAD_DIM), RNN_HEAD_DIM ** -0.5)
    rg_b = nrm(ks[7], (DEPTH, 2, D_RNN), 0.1)
    u = jax.random.uniform(ks[8], (DEPTH, D_RNN), f32, 0.9, 0.999)
    s_a = u ** (1.0 / LRU_C)
    a_param = jnp.log(s_a) - jnp.log1p(-s_a)
    w_out_conv = nrm(ks[9], (DEPTH, D_CONV, D_MODEL), D_CONV ** -0.5)
    w_out_rnn = nrm(ks[10], (DEPTH, D_RNN, D_MODEL), D_RNN ** -0.5)
    w_o = nrm(ks[11], (DEPTH, D_MODEL, D_MODEL), BETA * D_MODEL ** -0.5)
    ffn_w1 = nrm(ks[12], (DEPTH, 2, D_MODEL, 2 * D_FF), D_MODEL ** -0.5)
    ffn_w2 = nrm(ks[13], (DEPTH, 2, D_FF, D_MODEL), BETA * D_FF ** -0.5)
    ln_g = 1.0 + nrm(ks[14], (DEPTH, 3, D_MODEL), 0.02)
    ln_b = nrm(ks[15], (DEPTH, 3, D_MODEL), 0.02)
    return {"x": x, "w_in": w_in, "b_merge": b_merge, "sc_w": sc_w, "rc_w": rc_w,
            "rc_b": rc_b, "rg_w": rg_w, "rg_b": rg_b, "a_param": a_param,
            "w_out_conv": w_out_conv, "w_out_rnn": w_out_rnn, "w_o": w_o,
            "ffn_w1": ffn_w1, "ffn_w2": ffn_w2, "ln_g": ln_g, "ln_b": ln_b}

def first_block(x, w_in, b_merge, sc_w, rc_w, rc_b, rg_w, rg_b, a_param,
              w_out_conv, w_out_rnn, w_o, ffn_w1, ffn_w2, ln_g, ln_b):
    for l in range(DEPTH):
        x = layer_norm(ALPHA * x + 0.5 * swiglu(x, ffn_w1[l, 0], ffn_w2[l, 0]),
                       ln_g[l, 0], ln_b[l, 0])
        mix = hybrid_mixer(x, w_in[l], b_merge[l], sc_w[l], rc_w[l], rc_b[l], rg_w[l],
                           rg_b[l], a_param[l], w_out_conv[l], w_out_rnn[l], w_o[l])
        x = layer_norm(ALPHA * x + mix, ln_g[l, 1], ln_b[l, 1])
        x = layer_norm(ALPHA * x + 0.5 * swiglu(x, ffn_w1[l, 1], ffn_w2[l, 1]),
                       ln_g[l, 2], ln_b[l, 2])
    return x


CTX_LEN = 256
GRID_W = 64
NORM_EPS = 1e-6

HY_WIDTH = 1024
HY_SHORT = 3
HY_EMB = 33
HY_BANDS = (HY_EMB - 1) // 2
HY_HIDDEN = 64
HY_TARGET = 1e-2
HY_SHORT_DECAY_PCT = 0.3
HY_LONG_DECAY_PCT = 1.5

ATT_HEADS = 8
ATT_KV_HEADS = 2
HEAD_DIM = 128
ATT_WIDTH = ATT_HEADS * HEAD_DIM
Q_BLOCK = 128
ROPE_THETA = 10000.0

EVEN_MIX = HY_WIDTH + ATT_WIDTH
EVEN_SPLITS = (3 * HY_WIDTH, HY_WIDTH, ATT_WIDTH, ATT_KV_HEADS * HEAD_DIM, ATT_KV_HEADS * HEAD_DIM, ATT_WIDTH)
EVEN_IN = sum(EVEN_SPLITS)

ML_HEADS = 8
ML_QK = 128
ML_V = 256
ML_WIDTH = ML_HEADS * ML_V
ML_CHUNK = 64
ML_SHORT = 3
ODD_SPLITS = (ML_HEADS * ML_QK, ML_HEADS * ML_QK, ML_WIDTH, ML_WIDTH, ML_WIDTH, 4 * ML_HEADS)
ODD_IN = sum(ODD_SPLITS)

N_EVEN = (DEPTH + 1) // 2
N_ODD = DEPTH // 2


def _split(a, sizes):
    out, start = [], 0
    for s in sizes:
        out.append(a[..., start:start + s])
        start += s
    return out

def rms_norm(x, g):
    xf = x.astype(jnp.float32)
    y = xf * lax.rsqrt(jnp.mean(xf * xf, axis=-1, keepdims=True) + NORM_EPS)
    return (y * g.astype(jnp.float32)).astype(x.dtype)

def dw_conv(u, w, b):
    ch = u.shape[-1]
    k = w.shape[0]
    y = lax.conv_general_dilated(u, w[:, None, :].astype(u.dtype), window_strides=(1,),
                                 padding=[(k // 2, k // 2)], dimension_numbers=('NWC', 'WIO', 'NWC'),
                                 feature_group_count=ch)
    return y + b.astype(u.dtype)

def adaln(cond, w_mod, b_mod):
    m = jax.nn.silu(cond) @ w_mod + b_mod
    return _split(m, (D_MODEL, D_MODEL, D_MODEL))

def axial_rope(x, rows, cols):
    f32 = jnp.float32
    half = x.shape[-1] // 2
    nf = half // 2
    inv = ROPE_THETA ** (-jnp.arange(nf, dtype=f32) / nf)

    def rot(xa, pos):
        ang = pos.astype(f32)[:, None] * inv
        cos = jnp.cos(ang)[None, :, None, :]
        sin = jnp.sin(ang)[None, :, None, :]
        x1 = xa[..., :nf].astype(f32)
        x2 = xa[..., nf:].astype(f32)
        return jnp.concatenate([x1 * cos - x2 * sin, x1 * sin + x2 * cos], axis=-1)

    out = jnp.concatenate([rot(x[..., :half], rows), rot(x[..., half:], cols)], axis=-1)
    return out.astype(x.dtype)

def hyena_filter(n, w1, b1, freq, w2, b2, w3):
    f32 = jnp.float32
    t = jnp.linspace(0.0, 1.0, n, dtype=f32)[:, None]
    bands = jnp.linspace(1e-4, HY_BANDS - 1, HY_BANDS, dtype=f32)
    ang = (2.0 * math.pi / n) * jnp.arange(n, dtype=f32)[:, None] * bands
    z = jnp.concatenate([t, jnp.cos(ang), -jnp.sin(ang)], axis=-1)
    fr = freq.astype(f32)
    hdn = jnp.sin(fr * (z @ w1.astype(f32) + b1.astype(f32)))
    hdn = jnp.sin(fr * (hdn @ w2.astype(f32) + b2.astype(f32)))
    h = (hdn @ w3.astype(f32)).reshape(n, 2, HY_WIDTH)
    max_decay = math.log(HY_TARGET) / HY_SHORT_DECAY_PCT
    min_decay = math.log(HY_TARGET) / HY_LONG_DECAY_PCT
    deltas = jnp.linspace(min_decay, max_decay, HY_WIDTH, dtype=f32)
    h = h * jnp.exp(-t * jnp.abs(deltas))[:, None, :]
    two_sided = jnp.concatenate([h[:, 0], jnp.zeros((1, HY_WIDTH), f32), h[:0:-1, 1]], axis=0)
    return two_sided / jnp.sum(jnp.abs(two_sided), axis=0, keepdims=True)

def bidir_long_conv(u, filt):
    n = u.shape[1]
    uf = jnp.fft.rfft(u.astype(jnp.float32), n=2 * n, axis=1)
    ff = jnp.fft.rfft(filt, axis=0)
    return jnp.fft.irfft(uf * ff[None], n=2 * n, axis=1)[:, :n].astype(u.dtype)

def hyena_mixer(xv, conv_w, conv_b, f_w1, f_b1, f_freq, f_w2, f_b2, f_w3, hy_bias):
    n = xv.shape[1]
    x0, x1, v = _split(dw_conv(xv, conv_w, conv_b), (HY_WIDTH, HY_WIDTH, HY_WIDTH))
    filt = hyena_filter(n, f_w1, f_b1, f_freq, f_w2, f_b2, f_w3)
    g = v * x1
    return x0 * (bidir_long_conv(g, filt) + g * hy_bias.astype(g.dtype))

def block_attention(q, k, v):
    B, n, H, Dh = q.shape
    kvh = k.shape[2]
    grp = H // kvh
    nb = n // Q_BLOCK
    qb = jnp.moveaxis(q.reshape(B, nb, Q_BLOCK, kvh, grp, Dh), 1, 0)
    scale = Dh ** -0.5

    def attend(qblk):
        s = jnp.einsum('bqkgd,btkd->bkgqt', qblk, k, preferred_element_type=jnp.float32) * scale
        p = jax.nn.softmax(s, axis=-1).astype(v.dtype)
        return jnp.einsum('bkgqt,btkd->bqkgd', p, v)

    out = lax.map(attend, qb)
    return jnp.moveaxis(out, 0, 1).reshape(B, n, H * Dh)

def even_mixer(h_lat, h_ctx, rows, cols, need_ctx, w_in, conv_w, conv_b, f_w1, f_b1, f_freq,
               f_w2, f_b2, f_w3, hy_bias, q_norm, k_norm, w_out):
    def project(h):
        B, n = h.shape[:2]
        xv, g_hy, q, k, v, g_att = _split(h @ w_in, EVEN_SPLITS)
        q = rms_norm(q.reshape(B, n, ATT_HEADS, HEAD_DIM), q_norm)
        k = rms_norm(k.reshape(B, n, ATT_KV_HEADS, HEAD_DIM), k_norm)
        v = v.reshape(B, n, ATT_KV_HEADS, HEAD_DIM)
        return xv, g_hy, q, k, v, g_att

    def hyena(xv):
        return hyena_mixer(xv, conv_w, conv_b, f_w1, f_b1, f_freq, f_w2, f_b2, f_w3, hy_bias)

    def combine(hy, att, g_hy, g_att):
        return jnp.concatenate([hy * jax.nn.silu(g_hy), att * jax.nn.silu(g_att)], axis=-1) @ w_out

    xv_l, gh_l, q_l, k_l, v_l, ga_l = project(h_lat)
    xv_c, gh_c, q_c, k_c, v_c, ga_c = project(h_ctx)
    q_l = axial_rope(q_l, rows, cols)
    k_l = axial_rope(k_l, rows, cols)
    att_l = block_attention(q_l, jnp.concatenate([k_l, k_c], axis=1), jnp.concatenate([v_l, v_c], axis=1))
    y_lat = combine(hyena(xv_l), att_l, gh_l, ga_l)
    y_ctx = None
    if need_ctx:
        y_ctx = combine(hyena(xv_c), block_attention(q_c, k_c, v_c), gh_c, ga_c)
    return y_lat, y_ctx

def mlstm_chunkwise(q, k, v, i_pre, f_pre, state):
    f32 = jnp.float32
    B, H, n, _ = q.shape
    nc = n // ML_CHUNK

    def chunks(a):
        a = a.astype(f32)
        return jnp.moveaxis(a.reshape(B, H, nc, ML_CHUNK, *a.shape[3:]), 2, 0)

    lower = jnp.tril(jnp.ones((ML_CHUNK, ML_CHUNK), dtype=bool))

    def step(carry, inp):
        C, nvec, m = carry
        qc, kc, vc, ic, lfc = inp
        b = jnp.cumsum(lfc, axis=-1)
        d = jnp.where(lower, b[..., :, None] - b[..., None, :] + ic[..., None, :], -jnp.inf)
        inter = b + m[..., None]
        m_row = jnp.maximum(inter, jnp.max(d, axis=-1))
        s = jnp.einsum('bhtd,bhsd->bhts', qc, kc) * jnp.exp(d - m_row[..., None])
        w_prev = jnp.exp(inter - m_row)
        num = jnp.einsum('bhts,bhsv->bhtv', s, vc) + w_prev[..., None] * jnp.einsum('bhvd,bhtd->bhtv', C, qc)
        den = jnp.sum(s, axis=-1) + w_prev * jnp.einsum('bhd,bhtd->bht', nvec, qc)
        h = num / jnp.maximum(jnp.abs(den), jnp.exp(-m_row))[..., None]
        b_end = b[..., -1]
        g = b_end[..., None] - b + ic
        m_new = jnp.maximum(b_end + m, jnp.max(g, axis=-1))
        a = jnp.exp(g - m_new[..., None])
        a_prev = jnp.exp(b_end + m - m_new)
        C = a_prev[..., None, None] * C + jnp.einsum('bhsv,bhsd->bhvd', vc * a[..., None], kc)
        nvec = a_prev[..., None] * nvec + jnp.einsum('bhs,bhsd->bhd', a, kc)
        return (C, nvec, m_new), h

    xs = (chunks(q), chunks(k), chunks(v), chunks(i_pre), chunks(jax.nn.log_sigmoid(f_pre.astype(f32))))
    state, hs = lax.scan(step, state, xs)
    return state, jnp.moveaxis(hs, 0, 2).reshape(B, H, n, v.shape[-1])

def odd_mixer(h_lat, h_ctx, need_ctx, w_in, conv_w, conv_b, gate_b, head_norm, w_out):
    f32 = jnp.float32

    def project(h):
        B, n = h.shape[:2]
        q, k, v, o, z, gates = _split(h @ w_in, ODD_SPLITS)
        qk = jax.nn.silu(dw_conv(jnp.concatenate([q, k], axis=-1), conv_w, conv_b))
        q, k = _split(qk, (ML_HEADS * ML_QK, ML_HEADS * ML_QK))
        q = q.reshape(B, n, ML_HEADS, ML_QK).transpose(0, 2, 1, 3)
        k = k.reshape(B, n, ML_HEADS, ML_QK).transpose(0, 2, 1, 3) * (ML_QK ** -0.5)
        v = v.reshape(B, n, ML_HEADS, ML_V).transpose(0, 2, 1, 3)
        gates = (gates + gate_b).astype(f32).reshape(B, n, 4, ML_HEADS).transpose(2, 0, 3, 1)
        return q, k, v, o, z, gates

    def flip(a):
        return jnp.flip(a, axis=2)

    ql, kl, vl, ol, zl, gl = project(h_lat)
    qc, kc, vc, oc, zc, gc = project(h_ctx)
    B = h_lat.shape[0]
    zero = (jnp.zeros((B, ML_HEADS, ML_V, ML_QK), f32), jnp.zeros((B, ML_HEADS, ML_QK), f32),
            jnp.zeros((B, ML_HEADS), f32))
    st_f, hc_f = mlstm_chunkwise(qc, kc, vc, gc[0], gc[1], zero)
    _, hl_f = mlstm_chunkwise(ql, kl, vl, gl[0], gl[1], st_f)
    st_b, hc_b = mlstm_chunkwise(flip(qc), flip(kc), flip(vc), flip(gc[2]), flip(gc[3]), zero)
    _, hl_b = mlstm_chunkwise(flip(ql), flip(kl), flip(vl), flip(gl[2]), flip(gl[3]), st_b)

    def finish(h_f, h_b, o, z):
        Bn, _, n, _ = h_f.shape
        h = (h_f + h_b).transpose(0, 2, 1, 3).reshape(Bn, n, ML_WIDTH).astype(o.dtype) * jax.nn.sigmoid(o)
        h = rms_norm(h.reshape(Bn, n, ML_HEADS, ML_V), head_norm.reshape(ML_HEADS, ML_V)).reshape(Bn, n, ML_WIDTH)
        return (h * jax.nn.silu(z)) @ w_out

    y_lat = finish(hl_f, flip(hl_b), ol, zl)
    y_ctx = finish(hc_f, flip(hc_b), oc, zc) if need_ctx else None
    return y_lat, y_ctx

def second_inputs(seed: int = 0) -> dict:
    key = jax.random.key(seed)
    keys = jax.random.split(key, 32)
    f32 = jnp.float32

    def nrm(i, shape, scale):
        return jax.random.normal(keys[i], shape, f32) * scale

    D = D_MODEL
    forget_init = jnp.linspace(3.0, 6.0, ML_HEADS, dtype=f32)
    o_gate_b = jnp.concatenate([
        nrm(24, (N_ODD, ML_HEADS), 0.1),
        forget_init + nrm(25, (N_ODD, ML_HEADS), 0.1),
        nrm(26, (N_ODD, ML_HEADS), 0.1),
        forget_init + nrm(27, (N_ODD, ML_HEADS), 0.1)], axis=-1)
    return {
        'x': nrm(0, (BATCH, SEQ, D), 1.0),
        'c': nrm(1, (BATCH, D), 1.0),
        'ctx': nrm(2, (BATCH, CTX_LEN, D), 1.0),
        'c_ctx': nrm(3, (D,), 1.0),
        'w_mod': nrm(4, (DEPTH, D, 3 * D), D ** -0.5),
        'b_mod': nrm(5, (DEPTH, 3 * D), 0.02),
        'g_pre': 1.0 + nrm(6, (DEPTH, D), 0.02),
        'g_post': 1.0 + nrm(7, (DEPTH, D), 0.02),
        'e_w_in': nrm(8, (N_EVEN, D, EVEN_IN), D ** -0.5),
        'e_conv_w': nrm(9, (N_EVEN, HY_SHORT, 3 * HY_WIDTH), HY_SHORT ** -0.5),
        'e_conv_b': nrm(10, (N_EVEN, 3 * HY_WIDTH), 0.02),
        'e_filt_w1': nrm(11, (N_EVEN, HY_EMB, HY_HIDDEN), HY_EMB ** -0.5),
        'e_filt_b1': nrm(12, (N_EVEN, HY_HIDDEN), 0.1),
        'e_filt_freq': 1.0 + nrm(13, (N_EVEN, HY_HIDDEN), 0.02),
        'e_filt_w2': nrm(14, (N_EVEN, HY_HIDDEN, HY_HIDDEN), HY_HIDDEN ** -0.5),
        'e_filt_b2': nrm(15, (N_EVEN, HY_HIDDEN), 0.1),
        'e_filt_w3': nrm(16, (N_EVEN, HY_HIDDEN, 2 * HY_WIDTH), HY_HIDDEN ** -0.5),
        'e_hy_bias': nrm(17, (N_EVEN, HY_WIDTH), 0.1),
        'e_q_norm': 1.0 + nrm(18, (N_EVEN, HEAD_DIM), 0.02),
        'e_k_norm': 1.0 + nrm(19, (N_EVEN, HEAD_DIM), 0.02),
        'e_w_out': nrm(20, (N_EVEN, EVEN_MIX, D), EVEN_MIX ** -0.5),
        'o_w_in': nrm(21, (N_ODD, D, ODD_IN), D ** -0.5),
        'o_conv_w': nrm(22, (N_ODD, ML_SHORT, 2 * ML_HEADS * ML_QK), ML_SHORT ** -0.5),
        'o_conv_b': nrm(23, (N_ODD, 2 * ML_HEADS * ML_QK), 0.02),
        'o_gate_b': o_gate_b,
        'o_head_norm': 1.0 + nrm(28, (N_ODD, ML_WIDTH), 0.02),
        'o_w_out': nrm(29, (N_ODD, ML_WIDTH, D), ML_WIDTH ** -0.5),
    }

def second_block(x, c, ctx, c_ctx, w_mod, b_mod, g_pre, g_post, e_w_in, e_conv_w, e_conv_b, e_filt_w1,
              e_filt_b1, e_filt_freq, e_filt_w2, e_filt_b2, e_filt_w3, e_hy_bias, e_q_norm, e_k_norm,
              e_w_out, o_w_in, o_conv_w, o_conv_b, o_gate_b, o_head_norm, o_w_out):
    n_lat = x.shape[1]
    ROWS = n_lat // GRID_W
    rows = jnp.repeat(jnp.arange(ROWS, dtype=jnp.int32), GRID_W)
    cols = jnp.tile(jnp.arange(GRID_W, dtype=jnp.int32), ROWS)
    x_lat, x_ctx = x, ctx
    for layer in range(DEPTH):
        need_ctx = layer < DEPTH - 1
        sh_l, sc_l, ga_l = adaln(c, w_mod[layer], b_mod[layer])
        sh_c, sc_c, ga_c = adaln(c_ctx, w_mod[layer], b_mod[layer])
        h_lat = rms_norm(x_lat, g_pre[layer]) * (1 + sc_l[:, None]) + sh_l[:, None]
        h_ctx = rms_norm(x_ctx, g_pre[layer]) * (1 + sc_c) + sh_c
        j = layer // 2
        if layer % 2 == 0:
            y_lat, y_ctx = even_mixer(h_lat, h_ctx, rows, cols, need_ctx, e_w_in[j], e_conv_w[j], e_conv_b[j],
                                      e_filt_w1[j], e_filt_b1[j], e_filt_freq[j], e_filt_w2[j], e_filt_b2[j],
                                      e_filt_w3[j], e_hy_bias[j], e_q_norm[j], e_k_norm[j], e_w_out[j])
        else:
            y_lat, y_ctx = odd_mixer(h_lat, h_ctx, need_ctx, o_w_in[j], o_conv_w[j], o_conv_b[j], o_gate_b[j],
                                     o_head_norm[j], o_w_out[j])
        x_lat = x_lat + ga_l[:, None] * rms_norm(y_lat, g_post[layer])
        if need_ctx:
            x_ctx = x_ctx + ga_c * rms_norm(y_ctx, g_post[layer])
    return x_lat


def setup_inputs(seed=0):
    out = dict(first_inputs(seed))
    for name, value in second_inputs(seed + 1).items():
        if name != "x":
            out[name + "_2"] = value
    return out


def reference(
    x, w_in, b_merge, sc_w, rc_w, rc_b, rg_w, rg_b, a_param, w_out_conv, w_out_rnn, w_o, ffn_w1,
    ffn_w2, ln_g, ln_b, c_2, ctx_2, c_ctx_2, w_mod_2, b_mod_2, g_pre_2, g_post_2, e_w_in_2,
    e_conv_w_2, e_conv_b_2, e_filt_w1_2, e_filt_b1_2, e_filt_freq_2, e_filt_w2_2, e_filt_b2_2,
    e_filt_w3_2, e_hy_bias_2, e_q_norm_2, e_k_norm_2, e_w_out_2, o_w_in_2, o_conv_w_2,
    o_conv_b_2, o_gate_b_2, o_head_norm_2, o_w_out_2,
):
    x = first_block(
        x, w_in, b_merge, sc_w, rc_w, rc_b, rg_w, rg_b, a_param, w_out_conv, w_out_rnn, w_o,
        ffn_w1, ffn_w2, ln_g, ln_b,
    )
    return second_block(
        x, c_2, ctx_2, c_ctx_2, w_mod_2, b_mod_2, g_pre_2, g_post_2, e_w_in_2, e_conv_w_2,
        e_conv_b_2, e_filt_w1_2, e_filt_b1_2, e_filt_freq_2, e_filt_w2_2, e_filt_b2_2,
        e_filt_w3_2, e_hy_bias_2, e_q_norm_2, e_k_norm_2, e_w_out_2, o_w_in_2, o_conv_w_2,
        o_conv_b_2, o_gate_b_2, o_head_norm_2, o_w_out_2,
    )


_drawn_inputs = setup_inputs


def setup_inputs(seed=0):
    import zlib

    import numpy as np

    out = dict(_drawn_inputs(seed))
    spreads = {}
    factors = {'b_merge': 4.488,
     'rc_b': 3.362,
     'rg_b': 8.0,
     'g_pre_2': 3.146,
     'g_post_2': 3.855,
     'e_conv_b_2': 5.447,
     'e_filt_freq_2': 8.0,
     'e_q_norm_2': 8.0,
     'e_k_norm_2': 8.0,
     'o_conv_b_2': 60.568,
     'o_head_norm_2': 23.979}
    for name, (base, spread) in spreads.items():
        noise = np.random.default_rng([zlib.crc32(name.encode()), seed]).standard_normal(out[name].shape)
        drawn = base * np.exp(spread * noise) if base else spread * noise
        out[name] = jnp.asarray(drawn.astype(out[name].dtype))
    for name, factor in factors.items():
        out[name] = (out[name] * factor).astype(out[name].dtype)
    return out
```

```python
from contextlib import ExitStack

import concourse.bass as bass
import numpy as np
from concourse import mybir

F32 = mybir.dt.float32
I32 = mybir.dt.int32
F32R = mybir.dt.float32r
ACT = mybir.ActivationFunctionType
ALU = mybir.AluOpType

P = 128
D = 1024
KT = D // P
SEQ = 256
RT = SEQ // P
DEPTH = 2
D_FF = 2816
FT = D_FF // P
FJ = FT // 2
HEADS = 4
LRU_C = 8.0
ALPHA = (2.0 * DEPTH) ** 0.25
LN_EPS = 1e-5
BLK = KT * 512
RING = 4
W2_UNITS = 2 * FT
W2_BLOCKS = -(-W2_UNITS // KT)
HALF = BLK // 2
UP_HALVES = 2 * FJ
DOWN_HALVES = W2_UNITS // 4
assert W2_UNITS % 4 == 0

LCOL = {}
_at = 0
for _name, _n in (("ln_g", 24), ("ln_b", 24), ("b_merge", 16), ("sc_w", 24), ("rc_w", 32),
                  ("rc_b", 8), ("rg_b", 16), ("a_param", 8)):
    LCOL[_name] = _at
    _at += _n
LCOLS = _at
TWO_PI = 2.0 * np.pi
MAGIC = 1.5 * 2.0 ** 23
PI_BELOW = 3.1415925
TWO_PI_PARTS = (6.28125, 0.0019350051879882812, float(np.float32(TWO_PI - 6.28125 - 0.0019350051879882812)))

ROWS = 2 * SEQ
GRID_W = 64
NORM_EPS = 1e-6
HY_EMB, HY_HIDDEN = 33, 64
HY_TARGET, HY_SHORT_DECAY, HY_LONG_DECAY = 1e-2, 0.3, 1.5
Q_HEADS, KV_HEADS, HD = 8, 2, 128
ROPE_THETA = 10000.0
ML_HEADS, ML_V = 8, 256
HYC = 13
MLC = 10
MASKED = 1e30
C2 = {}
_at = 0
for _name, _n in (("cond", 2 * KT), ("b_mod", 96), ("g_pre", 32), ("g_post", 32), ("hy", KT * HYC), ("qk", 2),
                  ("ml", ML_HEADS * MLC), ("gate_b", 2)):
    C2[_name] = _at
    _at += _n
C2COLS = _at
CR = {}
_at = 0
for _name, _n in (("ident", P), ("ones", P), ("perm", P), ("mask", 2 * P), ("cos", SEQ), ("sin", SEQ)):
    CR[_name] = _at
    _at += _n
CRCOLS = _at
HYW = 4 * 512 + 256
FILTCOLS = SEQ + 2 * HY_HIDDEN + 2 * D + 4

L_FFN = FJ + W2_BLOCKS
L_MIX = 2 * HEADS + 2 + 6 + 2 + 2 + 2
L_BLOCKS = 2 * L_FFN + L_MIX
assert L_BLOCKS % RING == 0
AT_FFN = (0, L_FFN + L_MIX)
AT_MIX = L_FFN


def plan_layer():
    uses, count, pair = {}, [0] * 4, [0]

    def pair_use(*key):
        for side in range(2):
            bank = 2 * pair[0] + side
            uses[key + (side,)] = (bank, count[bank])
            count[bank] += 1
        pair[0] ^= 1

    def turn_use(n):
        for bank in range(4):
            uses["turn", n, bank] = (bank, count[bank])
            count[bank] += 1

    for n in range(3):
        for r in range(RT):
            uses["y", n, r] = (4 + 2 * r, n)
    for j in range(FJ):
        pair_use("up", 0, j)
    turn_use(0)
    for h in range(HEADS):
        pair_use("bc", h)
        pair_use("vx", h)
    for h in range(HEADS):
        pair_use("rg", h)
    for q in range(6):
        pair_use("yg", q)
    for q in range(2):
        pair_use("oc", q)
    for q in range(2):
        pair_use("or", q)
    turn_use(1)
    for j in range(FJ):
        pair_use("up", 1, j)
    turn_use(2)
    assert len(set(count)) == 1 and pair[0] == 0
    return uses


def in_turn(*keyed):
    uses, count = {}, [0] * 8
    for *key, bank in keyed:
        uses[tuple(key)] = (bank, count[bank])
        count[bank] += 1
    return uses


def plan_banks():
    heads = []
    for a in range(2):
        heads += [("qs", a, 4), ("qr", a, 5), ("s", a, 0, 6), ("s", a, 1, 7), ("s", a, 2, 6), ("s", a, 3, 7),
                  ("pt", a, 0, 4), ("pt", a, 1, 5), ("pt", a, 2, 6), ("o", a, 7)]
    segments = {
        "start": (1, in_turn(*[("turn", b, b) for b in range(4)])),
        "layer": (DEPTH, plan_layer()),
        "mod": (3, in_turn(("mod", 0), *[("row", u, 4 + u) for u in range(4)])),
        "even": (1, in_turn(
            ("f1", 1), ("f2", 2), *[("f3", t, q, 4 * t + q) for t in range(2) for q in range(4)],
            *[("pre", k, k) for k in range(KT)], ("fn", 0),
            *[("sp", p, h, (2 * p + h) % 8) for p in range(5) for h in range(2)],
            *[("gg", w, h, 4 + 2 * w + h) for w in range(2) for h in range(2)],
        )),
        "hyena": (KT, in_turn(("x", 0, 0), ("x", 1, 1), ("x", 2, 2), ("g", 3), ("ht", 4), ("ur", 5), ("ui", 6),
                              ("hc", 7))),
        "kv": (1, in_turn(("k", 0, 0), ("k", 1, 1), ("v", 0, 2), ("v", 1, 3), ("kss", 0, 4), ("kss", 1, 5),
                          ("kr", 0, 6), ("kr", 1, 7))),
        "heads": (Q_HEADS // 2, in_turn(("q", 0, 0), ("q", 1, 1), ("g", 0, 2), ("g", 1, 3), *heads)),
        "even_y": (1, in_turn(*[("y", h, r, 4 * (1 - h) + r) for h in range(2) for r in range(4)])),
        "odd": (1, in_turn(*[("pre", k, k) for k in range(KT)], ("gi", 0), ("gf", 1), ("gg", 0, 4), ("gg", 1, 5),
                           ("ct", 6), ("em", 7))),
        "ml": (ML_HEADS, in_turn(("q", 0), ("k", 1), ("v", 0, 2), ("v", 1, 3), ("o", 0), ("z", 1), ("mb", 4),
                                 ("s", 0, 5), ("s", 1, 6), ("n", 0, 0, 7), ("n", 0, 1, 4), ("n", 1, 0, 5),
                                 ("n", 1, 1, 6), ("t", 7))),
        "odd_y": (1, in_turn(*[("y", r, h, 4 + 2 * r + h) for r in range(RT) for h in range(2)])),
    }
    count = [0] * 8
    table = {}
    for name, (times, uses) in segments.items():
        per = [sum(b == bank for bank, _ in uses.values()) for b in range(8)]
        table[name] = {key: (bank, count[bank] + n, per[bank]) for key, (bank, n) in uses.items()}
        count = [c + times * p for c, p in zip(count, per)]
    return table


def build(nc, weights, cols, lnrows, consts, cols2, hy_consts, filt, gate_w, ctx_rows, x, out):
    plan = plan_banks()
    n_blocks = weights.shape[0]
    with ExitStack() as ctx:
        def sb(name, shape, dt=F32):
            return ctx.enter_context(nc.sbuf_tensor(name, shape, dt))

        def sem(name):
            return ctx.enter_context(nc.semaphore(name))

        def sharing(*areas):
            with ExitStack() as scope:
                parts = []
                for n, a in enumerate(areas):
                    if isinstance(a, int):
                        scope.enter_context(nc.sbuf_tensor(f"gap_before_{areas[n + 1][0]}", [P, a], F32))
                    else:
                        parts.append(scope.enter_context(nc.sbuf_tensor(a[0], a[1], F32R)))
            return parts

        ring = sb("ring", [P, RING, KT, 512])
        (x_lo,) = sharing(RT * D, ("x_lo", [P, KT, SEQ]))
        xrow = sb("xrow", [P, 4, D])
        (x_hi,) = sharing(KT * SEQ, ("x_hi", [P, KT, SEQ]))
        xt = sb("xt", [P, KT, 512])
        xt_flat = xt[:].rearrange("p k n -> p (k n)")
        xs = xt_flat[:, 0:KT * SEQ].rearrange("p (k n) -> p k n", k=KT)
        z = sb("z", [P, RT, D])
        bcast = sb("bcast", [P, 2, D])
        colsb = sb("colsb", [P, DEPTH * LCOLS])
        lc = sb("lc", [P, LCOLS])
        half_b = sb("half_b", [P, 16])
        half_m = sb("half_m", [P, 16])
        decay = sb("decay", [P, KT])
        small = sb("small", [P, 64])
        stats = sb("stats", [P, RT, 2, 6])
        mv = sb("mv", [P, RT, 2])
        rstd = sb("rstd", [P, RT, 4])
        cr = sb("cr", [P, CRCOLS])
        ident, ones, perm = (cr[:, CR[n]:CR[n] + P] for n in ("ident", "ones", "perm"))
        mask = cr[:, CR["mask"]:CR["mask"] + 2 * P].rearrange("p (d n) -> p d n", d=2)
        cos, sin = (cr[:, CR[n]:CR[n] + SEQ] for n in ("cos", "sin"))
        c2 = sb("c2", [P, C2COLS])
        cond = sb("cond", [P, KT, 2])
        mod = sb("mod", [P, 2, 24, 2])
        gain = sb("gain", [P, 2, KT, 2])
        gcol = sb("gcol", [P, 2, KT, 2])
        rs = sb("rs", [P, 48])
        hyc = sb("hyc", [P, 16])
        cv_pad = sb("cv_pad", [P, 2, 2 + SEQ])
        xr_pad = sb("xr_pad", [P, 2, 3 + SEQ])
        gt_hi, gt_lo, w_hi, w_lo = sharing(("gt_hi", [P, FT, SEQ]), ("gt_lo", [P, FT, SEQ]), 1024,
                                           ("w_hi", [P, 2, HALF]), ("w_lo", [P, 2, HALF]))
        arena = sb("arena", [P, 20820])

        top = [0]

        def part(n, *dims):
            view = arena[:, top[0]:top[0] + n]
            top[0] += n
            if len(dims) == 2:
                view = view.rearrange("p (a b) -> p a b", a=dims[0])
            return view

        top[0] = 2 * FT * SEQ
        sg = part(1024, 2, 512)
        top[0] = 0
        c_sb = part(512, 2, SEQ)
        ctmp = part(1024, 4, SEQ)
        ut = part(2048, KT, SEQ)
        xct = part(2048, KT, SEQ)
        th_i = part(2048, KT, SEQ)
        th_r = part(2048, KT, SEQ)
        a_t = part(2048, KT, SEQ)
        gy = part(2048, KT, SEQ)
        th_g = part(4096, 2 * KT, SEQ)
        mt = xct

        top[0] = 0
        mixt = part(2 * KT * ROWS, 2 * KT, ROWS)
        spec = part(5 * D, 5, D)
        hyw = part(HYW)
        tail = top[0]
        top[0] = 0
        mod_rows = arena[0:2, 0:4 * 512]
        f_sum, f_dif, f_abs, window = (part(2 * D, 2, D) for _ in range(4))
        top[0] = tail
        filt_sb = part(FILTCOLS)
        top[0] = tail
        diag = part(4608)[:, 4 * D:4 * D + 4 * P].rearrange("p (r n) -> p r n", r=4)
        top[0] = tail
        pad = part(3 * 2 * (SEQ + 2)).rearrange("p (c w n) -> p c w n", c=3, w=2)
        conved = part(3 * ROWS, 3, ROWS)
        hy_g = part(ROWS)
        hy_gt = part(4 * P, 4, P)
        prod = part(8 * P).rearrange("p (c k w n) -> p c k w n", c=2, k=2, w=2)
        z512 = z[:].rearrange("p r (h n) -> p (r h) n", h=2)
        top[0] = tail
        k_t = part(KV_HEADS * ROWS, KV_HEADS, ROWS)
        v_sb = part(4 * 256, 4, 256)
        q_sb = part(2 * ROWS, 2, ROWS)
        p_sb = part(4 * ROWS, 4, ROWS)[:, 0:2, :]
        top[0] = 2 * KT * ROWS
        pt_sb = part(6 * SEQ, 6, SEQ)
        th_a = part(2 * ROWS, 2, ROWS)
        tmp_a = part(4 * SEQ, 4, SEQ)
        dft_c, dft_s = (hyw[:, 512 * j:512 * (j + 1)].rearrange("p (t k) -> p t k", t=2) for j in range(2))
        idft = hyw[:, 1024:2048].rearrange("p (k t) -> p k t", k=4)
        dft_n = hyw[:, 2048:2304].rearrange("p (t k) -> p t k", t=2)
        hy_zt = filt_sb[0:HY_EMB, 0:SEQ]
        hy_w1 = filt_sb[0:HY_EMB, SEQ:SEQ + HY_HIDDEN]
        hy_w2 = filt_sb[0:HY_HIDDEN, SEQ + HY_HIDDEN:SEQ + 2 * HY_HIDDEN]
        hy_w3 = filt_sb[0:HY_HIDDEN, SEQ + 2 * HY_HIDDEN:FILTCOLS - 4]
        hyf = filt_sb[:, FILTCOLS - 4:FILTCOLS]

        top[0] = 0
        mt2 = part(2 * KT * SEQ, 2 * KT, SEQ)
        diag2 = arena[:, 0:4 * P].rearrange("p (r n) -> p r n", r=4)
        gw = part(2 * KT * 64).rearrange("p (g k n) -> p g k n", g=2, k=KT)
        g_i, g_b, g_c, g_m, g_t, g_u = (part(ROWS) for _ in range(6))
        c_t = part(4 * 64, 4, 64)
        em_t = part(RT * 64, RT, 64)
        ml_c = part(MLC + 8 + 4)
        q_pad = part(SEQ + 2)
        k_pad = part(2 * (SEQ + 2), 2, SEQ + 2)
        q_ml = part(SEQ)
        k_ml = part(ROWS)
        v_ml = part(4 * (ML_V + 1), 4, ML_V + 1)
        dec = part(2 * 4 * SEQ).rearrange("p (d k t) -> p d k t", d=2, k=4)
        dmask = part(2 * SEQ, 2, SEQ)
        p_ml = part(2 * 4 * SEQ).rearrange("p (d k t) -> p d k t", d=2, k=4)
        o_ml = part(RT * ML_V, RT, ML_V)
        h_ml = part(RT * ML_V, RT, ML_V)
        z_ml = part(2 * SEQ, 2, SEQ)
        t_ml = part(ROWS)
        den = part(32)

        banks = ctx.enter_context(nc.psum_tensor("banks", [P, 8, 512], F32))
        yacc = banks[:, 4:8, :].rearrange("p (r h) n -> p r (h n)", r=RT)

        wt_in = [sem(f"wt_in{s}") for s in range(RING)]
        wt_begun = sem("wt_begun")
        full = [sem(f"full{b}") for b in range(8)]
        free = [sem(f"free{b}") for b in range(8)]
        x_in = sem("x_in")
        c_in = sem("c_in")
        ready = sem("ready")
        row_in = sem("row_in")
        norm_done = sem("norm_done")
        xrow_done = sem("xrow_done")
        lc_done = sem("lc_done")
        xc_done = sem("xc_done")
        gate_done = sem("gate_done")
        m2_done = sem("m2_done")
        root_done = sem("root_done")
        hg_done = sem("hg_done")
        x_hi_done = sem("x_hi_done")
        x_split = sem("x_split")
        w_hi_done = sem("w_hi_done")
        w_lo_done = sem("w_lo_done")
        w_used = sem("w_used")
        m_done = sem("m_done")
        names = ("ctx_in", "hy_in", "gw_in", "cond_done", "diag_done", "ssq_done", "zz_done", "gain_done",
                 "sin_in", "sin_out", "f_done", "abs_in", "abs_out", "conv_done", "copied", "th_done", "hg_in",
                 "prod_done", "mix_done", "sq_done", "root2", "kn_done", "k_done", "qg_done", "rope_done", "row_ok",
                 "p_done", "pn_done", "post_ss", "post_done", "gates_done", "rows_done", "hc_done", "qk_conv", "qk_th",
                 "qk_done", "dm_done", "dec_done", "pml_done", "den_in", "ml_th", "ml_ss_in", "ml_ss", "hn_done",
                 "layer_done", "gate_exp", "gate_ab", "ct_in", "em_in", "t_done", "even_free")
        S2 = {name: sem(name) for name in names}
        sp_exp = sem("sp_exp")
        sp_abs = sem("sp_abs")
        out_done = sem("out_done")

        layer_uses = plan["layer"]["up", 0, 0, 0][2]
        block = ctx.enter_context(nc.Block())

        def uses_before(i, key):
            bank, n, per = plan[key[0]][key[1:]]
            return bank, (i * per + n if per else n)

        def take(pe, i, *key):
            bank, n = uses_before(i, key)
            pe.wait_ge(free[bank], n + 1)
            return bank

        def filled(eng, i, *key):
            bank, n = uses_before(i, key)
            eng.wait_ge(full[bank], n + 1)
            return bank

        def released(eng, i, *key):
            bank, n = uses_before(i, key)
            eng.wait_ge(free[bank], n + 2)

        def half_parts(h):
            def raw(slot):
                if h < UP_HALVES:
                    return ring[:, slot, :, (h % 2) * SEQ:(h % 2 + 1) * SEQ]
                return ring[:, slot, 4 * (h % 2):4 * (h % 2) + 4, :]

            if h < UP_HALVES:
                return (raw,) + tuple(w[:, h % 2].rearrange("p (k n) -> p k n", k=KT) for w in (w_hi, w_lo))
            return (raw,) + tuple(w[:, h % 2].rearrange("p (k n) -> p k n", k=4) for w in (w_hi, w_lo))

        def halves_before(l, f, h):
            return l * (2 * (UP_HALVES + DOWN_HALVES)) + f * (UP_HALVES + DOWN_HALVES) + h

        def split_used(eng, l, f, h):
            u = h - 2
            if u >= UP_HALVES:
                eng.wait_ge(w_used, l * (2 * (DOWN_HALVES - 1)) + (f * (DOWN_HALVES - 1) + u - UP_HALVES + 1))
            elif u >= 0:
                filled(eng, l, "layer", "up", f, u // 2, u % 2)

        @block.sync
        def _(sp):
            sp.dma_start(xrow[:, 0:RT, :], x.rearrange("o (r p) d -> p (o r) d", p=P)).then_inc(x_in, 16)
            sp.dma_start(cr[:], consts).then_inc(c_in, 16)
            sp.dma_start(c2[:], cols2).then_inc(c_in, 16)
            sp.dma_start(colsb[:], cols).then_inc(c_in, 16)
            for s in range(RING):
                sp.dma_start(ring[:, s], weights[s].rearrange("p (k n) -> p k n", k=KT)).then_inc(wt_in[s], 16)
            with sp.Fori(1, n_blocks // RING) as g:
                for s in range(RING):
                    sp.wait_ge(wt_begun, g * RING + (s + 2 - RING))
                    sp.dma_start(ring[:, s], weights[bass.ds(g * RING + s, 1)].rearrange(
                        "o p (k n) -> p (o k) n", k=KT)).then_inc(wt_in[s], 16)
            for n in range(n_blocks - n_blocks % RING, n_blocks):
                sp.wait_ge(wt_begun, n + 2 - RING)
                sp.dma_start(ring[:, n % RING], weights[n].rearrange("p (k n) -> p k n", k=KT)).then_inc(
                    wt_in[n % RING], 16)
            sp.wait_ge(S2["post_done"], 8 + 4)
            sp.dma_start(out.rearrange("o (r p) d -> p (o r) d", p=P), xrow[:, 0:RT, :]).then_inc(out_done, 16)
            sp.wait_ge(out_done, 16)

        @block.gpsimd
        def _(pool):
            nc.gpsimd.memset(cv_pad[:], 0.0).then_inc(ready, 1)
            nc.gpsimd.memset(xr_pad[:], 0.0).then_inc(ready, 1)
            for s in free:
                pool.sem_inc(s, 1)
            pool.wait_ge(x_in, 16)
            pool.sem_inc(xrow_done, 1)
            with pool.Fori(0, DEPTH) as l:
                for n in range(3):
                    for i in range(2):
                        pool.dma_start(bcast[:, i, :], lnrows[bass.ds(l * 6 + 2 * n + i, 1), :]
                                       .to_broadcast([P, D])).then_inc(row_in, 16)
                    pool.wait_ge(row_in, l * 96 + 32 * n + 32)
                    for r in range(RT):
                        pool.wait_ge(norm_done, l * 6 + RT * n + r + 1)
                        nc.gpsimd.tensor_tensor(xrow[:, r, :], z[:, r, :], bcast[:, 0, :], ALU.mult)
                        nc.gpsimd.drain()
                        nc.gpsimd.tensor_tensor(xrow[:, r, :], xrow[:, r, :], bcast[:, 1, :],
                                                ALU.add).then_inc(xrow_done, 1)
                    nc.gpsimd.drain()
            pool.wait_ge(norm_done, 6 * DEPTH)
            pool.dma_start(hyw[:], hy_consts[:, 0:HYW]).then_inc(S2["hy_in"], 16)
            pool.dma_start(window[:].rearrange("p a b -> p (a b)"), hy_consts[:, HYW:HYW + 2 * D])\
                .then_inc(S2["hy_in"], 16)
            pool.dma_start(filt_sb[0:HY_HIDDEN, :], filt).then_inc(S2["hy_in"], 16)
            pool.wait_ge(x_split, 2 * DEPTH + 1)
            pool.dma_start(xrow[:, RT:2 * RT, :], ctx_rows.rearrange("o (r p) d -> p (o r) d", p=P)).then_inc(
                S2["ctx_in"], 16)
            pool.wait_ge(S2["post_done"], 8)
            pool.dma_start(gw[:].rearrange("p g k n -> p (g k n)"), gate_w).then_inc(S2["gw_in"], 16)

        @block.tensor
        def _(pe):
            def slot_of(l, i):
                pe.wait_ge(wt_in[i % RING], l * (16 * L_BLOCKS // RING) + 16 * (i // RING + 1))
                return i % RING

            def begun(first, mm, blocks=1):
                if first:
                    mm.then_inc(wt_begun, blocks)

            def pair(l, i, rhs, *key, blocks=1):
                s = slot_of(l, i)
                side = [take(pe, l, "layer", *key, 0), take(pe, l, "layer", *key, 1)]
                for t in range(4):
                    b = side[t // 2]
                    for k in range(KT):
                        mm = nc.tensor.matmul(banks[:, b, (t % 2) * SEQ:(t % 2 + 1) * SEQ],
                                              ring[:, s, k, t * P:(t + 1) * P], rhs[:, k, 0:SEQ],
                                              start=k == 0, stop=k == KT - 1)
                        begun(t == 0 and k == 0, mm, blocks)
                    if t % 2:
                        mm.then_inc(full[b], 1)

            def turn(l, n):
                for r in range(RT):
                    pe.wait_ge(norm_done, l * 6 + RT * n + r + 1)
                    for b in range(4):
                        if r == 0:
                            take(pe, l, "layer", "turn", n, b)
                        for k in (2 * b, 2 * b + 1):
                            mm = nc.tensor.transpose(
                                banks[:, b, (k % 2) * SEQ + r * P:(k % 2) * SEQ + (r + 1) * P],
                                z[:, r, k * P:(k + 1) * P], ident)
                        if r == RT - 1:
                            mm.then_inc(full[b], 1)

            def xt_ready(l, n):
                for b in range(4):
                    if n == 0:
                        pe.wait_ge(free[b], l * layer_uses + 2)
                    else:
                        released(pe, l, "layer", "turn", n - 1, b)

            def rows(l, i, act_t, units, wait=None):
                for u0 in range(0, len(units), KT):
                    s = slot_of(l, i + u0 // KT)
                    for r in range(RT):
                        for j, (k, half, last_k) in enumerate(units[u0:u0 + KT]):
                            if wait:
                                wait(k, half, r)
                            mm = nc.tensor.matmul(yacc[:, r, half * 512:(half + 1) * 512],
                                                  act_t[:, k, r * P:(r + 1) * P], ring[:, s, j, :],
                                                  start=k == 0, stop=k == last_k)
                            begun(r == 0 and j == 0, mm)
                        if u0 + KT >= len(units):
                            mm.then_inc(full[4 + 2 * r], 1)

            def take_rows(l, n):
                for r in range(RT):
                    take(pe, l, "layer", "y", n, r)

            def ffn(l, f, n):
                xt_ready(l, n)
                pe.wait_ge(x_split, l * 2 + f + 1)
                for h in range(UP_HALVES):
                    j, side = h // 2, h % 2
                    if side == 0:
                        bs = [take(pe, l, "layer", "up", f, j, 0), take(pe, l, "layer", "up", f, j, 1)]
                    _, hi, lo = half_parts(h)
                    for t in range(2):
                        for low, parts in ((False, ((hi, x_hi), (hi, x_lo))), (True, ((lo, x_hi),))):
                            if t == 0:
                                pe.wait_ge(w_lo_done if low else w_hi_done, halves_before(l, f, h) + 1)
                            for k in range(KT):
                                for p, (w, x_) in enumerate(parts):
                                    mm = nc.tensor.matmul(banks[:, bs[side], t * SEQ:(t + 1) * SEQ],
                                                          w[:, k, t * P:(t + 1) * P], x_[:, k, :],
                                                          start=k == 0 and p == 0 and not low,
                                                          stop=k == KT - 1 and low)
                                    begun(side == 0 and not low and t == 0 and k == 0 and p == 0, mm)
                    mm.then_inc(full[bs[side]], 1)
                take_rows(l, n)
                for h in range(UP_HALVES, UP_HALVES + DOWN_HALVES):
                    _, hi, lo = half_parts(h)
                    u0 = 4 * (h - UP_HALVES)
                    for low, parts in ((False, ((gt_hi, hi), (gt_lo, hi))), (True, ((gt_hi, lo),))):
                        pe.wait_ge(w_lo_done if low else w_hi_done, halves_before(l, f, h) + 1)
                        for r in range(RT):
                            for u in range(4):
                                side, k = (u0 + u) // FT, (u0 + u) % FT
                                if side == 0 and r == 0 and k % 2 == 0 and not low:
                                    released(pe, l, "layer", "up", f, k // 2, 1)
                                for p, (g, w) in enumerate(parts):
                                    mm = nc.tensor.matmul(yacc[:, r, side * 512:(side + 1) * 512],
                                                          g[:, k, r * P:(r + 1) * P], w[:, u, :],
                                                          start=k == 0 and p == 0 and not low,
                                                          stop=k == FT - 1 and low)
                                    begun(h % 2 == 0 and not low and r == 0 and u == 0 and p == 0, mm)
                            if low and h == UP_HALVES + DOWN_HALVES - 1:
                                mm.then_inc(full[4 + 2 * r], 1)
                    if h < UP_HALVES + DOWN_HALVES - 1:
                        mm.then_inc(w_used, 1)

            pe.wait_ge(c_in, 48)
            pe.wait_ge(x_in, 16)
            for b in range(4):
                pe.wait_ge(free[b], 1)
            for r in range(RT):
                for k in range(KT):
                    mm = nc.tensor.transpose(banks[:, k // 2, (k % 2) * SEQ + r * P:(k % 2) * SEQ + (r + 1) * P],
                                             xrow[:, r, k * P:(k + 1) * P], ident)
                    if r == RT - 1 and k % 2:
                        mm.then_inc(full[k // 2], 1)

            with pe.Fori(0, DEPTH) as l:
                ffn(l, 0, 0)
                turn(l, 0)
                i = AT_MIX
                xt_ready(l, 1)
                for h in range(HEADS):
                    pair(l, i, xs, "bc", h)
                    pair(l, i + 1, xs, "vx", h)
                    i += 2
                s0, s1 = slot_of(l, i), slot_of(l, i + 1)
                for h in range(HEADS):
                    pe.wait_ge(xc_done, l * HEADS + h + 2)
                    for gate, s in ((0, s0), (1, s1)):
                        b = take(pe, l, "layer", "rg", h, gate)
                        w = ring[:, s].rearrange("p k n -> p (k n)")
                        for j in range(2):
                            for k in range(2):
                                c0 = (2 * h + k) * 256 + j * P
                                mm = nc.tensor.matmul(banks[:, b, j * SEQ:(j + 1) * SEQ], w[:, c0:c0 + P],
                                                      xct[:, 2 * h + k, :], start=k == 0, stop=k == 1)
                                begun(h == 0 and gate == 0 and j == 0 and k == 0, mm)
                        mm.then_inc(full[b], 1)
                i += 2
                for q in range(6):
                    pair(l, i + q, xs, "yg", q, blocks=1 + (q == 0))
                i += 6
                released(pe, l, "layer", "bc", HEADS - 1, 0)
                for q in range(2):
                    pair(l, i + q, ut, "oc", q)
                i += 2
                pe.wait_ge(hg_done, l + 1)
                for q in range(2):
                    pair(l, i + q, a_t, "or", q)
                i += 2
                take_rows(l, 1)
                pe.wait_ge(m_done, l * 4 + 4)
                rows(l, i, mt, [(k, half, KT - 1) for half in range(2) for k in range(KT)])
                turn(l, 1)
                ffn(l, 1, 2)
                turn(l, 2)

            at = [DEPTH * L_BLOCKS]

            def arrived(reps=None):
                n = at[0]
                at[0] += 1
                turns = n // RING + 1
                if reps is not None:
                    i, blocks = reps
                    pe.wait_ge(wt_in[n % RING], i * (16 * blocks // RING) + 16 * turns)
                else:
                    pe.wait_ge(wt_in[n % RING], 16 * turns)
                return n % RING

            def group(out, pairs, done=None, first=False):
                for n, (lhs, rhs) in enumerate(pairs):
                    mm = nc.tensor.matmul(out, lhs, rhs, start=n == 0, stop=n == len(pairs) - 1)
                    begun(first and n == 0, mm)
                if done is not None:
                    mm.then_inc(full[done], 1)
                return mm

            def tile_t(s, t, cols_n=ROWS):
                return [(ring[:, s, k, t * P:(t + 1) * P], xt[:, k, 0:cols_n]) for k in range(KT)]

            def tile_r(s, c0, c1, r):
                return [(xt[:, k, r * P:(r + 1) * P], ring[:, s, k, c0:c1]) for k in range(KT)]

            def turn_all(seg, src, layer):
                pe.wait_ge(S2["zz_done"], 4 * layer + 4)
                for k in range(KT):
                    take(pe, 0, seg, "pre", k)
                    for r in range(4):
                        mm = nc.tensor.matmul(banks[:, k, r * P:(r + 1) * P], xrow[:, r, k * P:(k + 1) * P],
                                              src[:, r, :], start=True, stop=True)
                    mm.then_inc(full[k], 1)

            pe.wait_ge(S2["cond_done"], 1)

            def modulation(i, loop):
                b = take(pe, i, "mod", "mod")

                def turn_rows(u):
                    released(pe, i, "mod", "row", u)
                    for t in range(4 * u, 4 * u + 4):
                        mm = group(banks[:, b, 2 * t:2 * t + 2], [(mod_rows[:, t * P:(t + 1) * P], ident[0:2, 0:2])])
                    return mm

                for u in range(4):
                    s = arrived((i, 4) if loop else None)
                    row = take(pe, i, "mod", "row", u)
                    group(banks[0:2, row, :], [(cond[:, k, :], ring[:, s, k, :]) for k in range(KT)], done=row,
                          first=True)
                    if u:
                        turn_rows(u - 1)
                turn_rows(3).then_inc(full[b], 1)

            start = at[0]
            with pe.Fori(0, 2) as i:
                modulation(i, True)
            at[0] = start + 8
            pe.wait_ge(S2["hy_in"], 48)
            b = take(pe, 0, "even", "f1")
            group(banks[0:HY_HIDDEN, b, 0:SEQ], [(hy_w1, hy_zt)], done=b)
            modulation(2, False)
            pe.wait_ge(S2["sin_out"], 1)
            b = take(pe, 0, "even", "f2")
            group(banks[0:HY_HIDDEN, b, 0:SEQ], [(hy_w2, z512[0:HY_HIDDEN, 0, 0:SEQ])], done=b)
            pe.wait_ge(S2["sin_out"], 2)
            for t in range(2):
                for q in range(4):
                    b = take(pe, 0, "even", "f3", t, q)
                    group(banks[:, b, :], [(z512[0:HY_HIDDEN, 1, t * P:(t + 1) * P], hy_w3[:, q * 512:(q + 1) * 512])],
                          done=b)
            turn_all("even", diag, 0)
            pe.wait_ge(S2["f_done"], 1)
            b = take(pe, 0, "even", "fn")
            for c in range(KT):
                mm = group(banks[:, b, c:c + 1], [(f_abs[:, t, c * P:(c + 1) * P], ones[:, 0:1]) for t in range(2)])
            mm.then_inc(full[b], 1)
            for p, (table, k0, src) in enumerate(((dft_c, 0, f_sum), (dft_n, 0, f_sum), (dft_c, 1, f_sum),
                                                  (dft_s, 0, f_dif), (dft_s, 1, f_dif))):
                for h in range(2):
                    b = take(pe, 0, "even", "sp", p, h)
                    group(banks[:, b, :], [(table[:, t, k0 * P:(k0 + 1) * P], src[:, t, h * 512:(h + 1) * 512])
                                           for t in range(2)], done=b)
            pe.wait_ge(S2["diag_done"], 1)
            for w in range(2):
                for h in range(2):
                    b = take(pe, 0, "even", "gg", w, h)
                    group(banks[:, b, :], [(ones, z[:, w, h * 512:(h + 1) * 512])], done=b)
            for k in range(KT):
                released(pe, 0, "even", "pre", k)
            def long_conv(i):
                pe.wait_ge(S2["prod_done"], i + 1)
                b = take(pe, i, "hyena", "hc")
                for w in range(2):
                    mm = group(banks[:, b, w * SEQ:(w + 1) * SEQ],
                               [(prod[:, p // 2, p % 2, w, :], idft[:, p, :]) for p in range(4)])
                mm.then_inc(full[b], 1)

            start = at[0]
            with pe.Fori(0, KT // RING) as i4:
                at[0] = start
                for u in range(RING):
                    i = i4 * RING + u
                    s = arrived((i4, RING))
                    for t, key in enumerate((("x", 0), ("x", 1), ("x", 2), ("g",))):
                        b = take(pe, i, "hyena", *key)
                        group(banks[:, b, :], tile_t(s, t), done=b, first=t == 0)
                        if t == 0 and u:
                            long_conv(i4 * RING + (u - 1))
                    pe.wait_ge(S2["hg_in"], i + 1)
                    b = take(pe, i, "hyena", "ht")
                    for r in range(4):
                        mm = nc.tensor.transpose(banks[:, b, r * P:(r + 1) * P], hy_g[:, r * P:(r + 1) * P], ident)
                    mm.then_inc(full[b], 1)
                    released(pe, i, "hyena", "ht")
                    gt4 = hy_gt[:].rearrange("p (w t) n -> p w t n", w=2)
                    for key, table in (("ur", dft_c), ("ui", dft_s)):
                        b = take(pe, i, "hyena", key)
                        for k in range(2):
                            mm = group(banks[:, b, k * SEQ:(k + 1) * SEQ].rearrange("p (w n) -> p w n", w=2),
                                       [(table[:, t, k * P:(k + 1) * P], gt4[:, :, t, :]) for t in range(2)])
                        mm.then_inc(full[b], 1)
                long_conv(i4 * RING + (RING - 1))
            at[0] = start + KT
            s = arrived()
            for t in range(2):
                b = take(pe, 0, "kv", "k", t)
                group(banks[:, b, :], tile_t(s, t), done=b, first=t == 0)
            for t in range(2):
                b = take(pe, 0, "kv", "v", t)
                for r in (2 * t, 2 * t + 1):
                    mm = group(banks[:, b, (r % 2) * 256:(r % 2 + 1) * 256], tile_r(s, 256, 512, r))
                mm.then_inc(full[b], 1)
            for t in range(2):
                pe.wait_ge(S2["sq_done"], t + 1)
                b = take(pe, 0, "kv", "kss", t)
                group(banks[:, b, :], [(ones, th_a[:, t, :])], done=b)
            for t in range(2):
                pe.wait_ge(S2["kn_done"], t + 1)
                b = take(pe, 0, "kv", "kr", t)
                group(banks[:, b, 0:SEQ], [(perm, k_t[:, t, 0:SEQ])], done=b)
            pe.wait_ge(S2["k_done"], 2)
            start = at[0]
            assert Q_HEADS // 2 == RING

            def project(i, s, t, half=None):
                key = (("q", 0), ("q", 1), ("g", 0), ("g", 1))[t]
                b = take(pe, i, "heads", *key) if not half else plan["heads"][key][0]
                c0, c1 = (0, ROWS) if half is None else (half * SEQ, (half + 1) * SEQ)
                group(banks[:, b, c0:c1], [(ring[:, s, k, t * P:(t + 1) * P], xt[:, k, c0:c1]) for k in range(KT)],
                      done=b if half != 0 else None, first=t == 0 and not half)

            s = arrived()
            project(0, s, 0)
            for i in range(Q_HEADS // 2):
                for a in range(2):
                    h = 2 * i + a
                    kv = h // (Q_HEADS // KV_HEADS)
                    more = i + 1 < Q_HEADS // 2
                    pe.wait_ge(S2["qg_done"], 2 * i + a + 1)
                    b = take(pe, i, "heads", "qs", a)
                    for r in range(4):
                        mm = group(banks[:, b, r:r + 1], [(tmp_a[:, 0:2, :].rearrange("p a b -> p (a b)")
                                                           [:, r * P:(r + 1) * P], ones[:, 0:1])])
                    mm.then_inc(full[b], 1)
                    b = take(pe, i, "heads", "qr", a)
                    group(banks[:, b, 0:SEQ], [(perm, q_sb[:, a, 0:SEQ])], done=b)
                    if a == 0:
                        project(i, s, 1)
                    else:
                        project(i, s, 3, 1)
                        if more:
                            s = arrived()
                    pe.wait_ge(S2["rope_done"], 2 * i + a + 1)
                    for r in range(4):
                        keys = k_t[:, kv, 0:ROWS] if r < RT else k_t[:, kv, SEQ:ROWS]
                        b = take(pe, i, "heads", "s", a, r)
                        group(banks[:, b, 0:keys.shape[-1]], [(q_sb[:, a, r * P:(r + 1) * P], keys)], done=b)
                        if r % 2:
                            if a == 0 and r == 1:
                                project(i, s, 2)
                            elif a == 0:
                                project(i, s, 3, 0)
                            elif more:
                                project(i + 1, s, 0, r // 2)
                            pe.wait_ge(S2["pn_done"], 8 * i + 4 * a + r + 1)
                            for j in ((0, 1) if r == 1 else (2,)):
                                b = take(pe, i, "heads", "pt", a, j)
                                for kt in range(2):
                                    for rr in range(2):
                                        src = p_sb[:, rr, (2 * j + kt) * P:(2 * j + kt + 1) * P] if j < 2 else \
                                            p_sb[:, rr, kt * P:(kt + 1) * P]
                                        c0 = kt * SEQ + rr * P
                                        mm = nc.tensor.transpose(banks[:, b, c0:c0 + P], src, ident)
                                mm.then_inc(full[b], 1)
                            if r == 1:
                                released(pe, i, "heads", "pt", a, 1)
                    for j in range(3):
                        released(pe, i, "heads", "pt", a, j)
                    b = take(pe, i, "heads", "o", a)
                    vh = v_sb[:, :, kv * HD:(kv + 1) * HD]
                    group(banks[:, b, 0:SEQ], [(vh[:, kt, :], pt_sb[:, kt, :]) for kt in range(4)])
                    group(banks[:, b, SEQ:ROWS], [(vh[:, 2 + kt, :], pt_sb[:, 4 + kt, :]) for kt in range(2)], done=b)
            pe.wait_ge(S2["mix_done"], KT + Q_HEADS)

            def out_rows(seg, src, tiles, key):
                for h in range(2):
                    bs = [take(pe, 0, seg, "y", *key(h, r)) for r in range(tiles)]
                    for half_k in range(2):
                        s = arrived()
                        for r in range(tiles):
                            for k in range(KT):
                                kk = KT * half_k + k
                                mm = nc.tensor.matmul(banks[:, bs[r], :], src[:, kk, r * P:(r + 1) * P], ring[:, s, k, :],
                                                      start=kk == 0, stop=kk == 2 * KT - 1)
                                begun(r == 0 and k == 0, mm)
                            if half_k:
                                mm.then_inc(full[bs[r]], 1)

            out_rows("even_y", mixt, 4, lambda h, r: (h, r))
            turn_all("odd", diag2, 1)
            for k in range(KT):
                released(pe, 0, "odd", "pre", k)
            pe.wait_ge(S2["gw_in"], 16)
            for g, key in enumerate(("gi", "gf")):
                b = take(pe, 0, "odd", key)
                group(banks[0:64, b, :], [(gw[:, g, k, :], xt[:, k, :]) for k in range(KT)], done=b)
            pe.wait_ge(S2["diag_done"], 2)
            for h in range(2):
                b = take(pe, 0, "odd", "gg", h)
                group(banks[:, b, :], [(ones, z[:, 0, h * 512:(h + 1) * 512])], done=b)

            def queries_keys(i):
                s = arrived()
                b = take(pe, i, "ml", "q")
                group(banks[:, b, 0:SEQ], tile_t(s, 0, SEQ), done=b, first=True)
                b = take(pe, i, "ml", "k")
                group(banks[:, b, :], tile_t(s, 1), done=b)
                return s

            def values(i, s):
                for t in range(2):
                    b = take(pe, i, "ml", "v", t)
                    for r in (2 * t, 2 * t + 1):
                        mm = group(banks[:, b, (r % 2) * 256:(r % 2 + 1) * 256], tile_r(s, 256, 512, r))
                    mm.then_inc(full[b], 1)

            values(0, queries_keys(0))
            pe.wait_ge(S2["ct_in"], 1)
            b = take(pe, 0, "odd", "ct")
            for j in range(4):
                mm = nc.tensor.transpose(banks[:, b, j * 64:(j + 1) * 64], g_c[0:64, j * P:(j + 1) * P], ident[0:64, 0:64])
            mm.then_inc(full[b], 1)
            pe.wait_ge(S2["em_in"], 1)
            b = take(pe, 0, "odd", "em")
            for r in range(RT):
                mm = nc.tensor.transpose(banks[:, b, r * 64:(r + 1) * 64], g_u[0:64, r * P:(r + 1) * P], ident[0:64, 0:64])
            mm.then_inc(full[b], 1)
            for i in range(ML_HEADS):
                s = arrived()
                b = take(pe, i, "ml", "o")
                for r in range(RT):
                    mm = group(banks[:, b, r * ML_V:(r + 1) * ML_V], tile_r(s, 0, 256, r), first=r == 0)
                mm.then_inc(full[b], 1)
                b = take(pe, i, "ml", "z")
                for t in range(2):
                    mm = group(banks[:, b, t * SEQ:(t + 1) * SEQ], tile_t(s, 2 + t, SEQ))
                mm.then_inc(full[b], 1)
                b = take(pe, i, "ml", "mb")
                for d, c0 in ((0, SEQ), (1, 0)):
                    sel = ident[0:64, 32 * d + i:32 * d + i + 1].to_broadcast([64, P])
                    mm = group(banks[:, b, d * SEQ:(d + 1) * SEQ], [(sel, g_m[0:64, c0:c0 + SEQ])])
                mm.then_inc(full[b], 1)
                pe.wait_ge(S2["qk_done"], i + 1)
                for half in range(2):
                    b = take(pe, i, "ml", "s", half)
                    for j in range(2):
                        kt = 2 * (1 - half) + j
                        mm = group(banks[:, b, j * SEQ:(j + 1) * SEQ], [(k_ml[:, kt * P:(kt + 1) * P], q_ml[:])])
                    mm.then_inc(full[b], 1)
                if i + 1 < ML_HEADS:
                    s = queries_keys(i + 1)
                released(pe, i, "ml", "v", 0)
                released(pe, i, "ml", "v", 1)
                for d in range(2):
                    pe.wait_ge(S2["pml_done"], 4 * i + 2 * d + 2)
                    for r in range(RT):
                        b = take(pe, i, "ml", "n", d, r)
                        own = [2 + j for j in range(2) if (j <= r if d == 0 else j >= r)]
                        group(banks[:, b, 0:ML_V + 1],
                              [(p_ml[:, d, kt, r * P:(r + 1) * P], v_ml[:, (kt + 2) % 4, :]) for kt in [0, 1] + own],
                              done=b)
                if i + 1 < ML_HEADS:
                    values(i + 1, s)
                pe.wait_ge(S2["hn_done"], 2 * i + 2)
                b = take(pe, i, "ml", "t")
                for t in range(2):
                    for r in range(RT):
                        mm = nc.tensor.transpose(banks[:, b, t * SEQ + r * P:t * SEQ + (r + 1) * P],
                                                 h_ml[:, r, t * P:(t + 1) * P], ident)
                mm.then_inc(full[b], 1)
            pe.wait_ge(S2["t_done"], 2 * ML_HEADS)
            out_rows("odd_y", mt2, RT, lambda h, r: (r, h))

        @block.scalar
        def _(act):
            def turned(l, n):
                for b in (0, 2):
                    filled(act, l, "layer", "turn", n, b)
                    for k in (2 * b, 2 * b + 1):
                        g0 = LCOL["ln_g"] + 8 * n + k
                        b0 = LCOL["ln_b"] + 8 * n + k
                        last = nc.scalar.activation(xs[:, k, :], banks[:, b, (k % 2) * SEQ:(k % 2 + 1) * SEQ],
                                                    ACT.Identity, scale=lc[:, g0:g0 + 1],
                                                    bias=lc[:, b0:b0 + 1])
                    last.then_inc(free[b], 1)
                    if n:
                        features_hi(b)

            def features_hi(b):
                nc.scalar.drain()
                nc.scalar.activation(x_hi[:, 2 * b:2 * b + 2, :], xs[:, 2 * b:2 * b + 2, :], ACT.Copy)\
                    .then_inc(x_hi_done, 1)

            def weights_hi(l, f, h):
                i = AT_FFN[f] + h // 2
                if h % 2 == 0:
                    act.wait_ge(wt_in[i % RING], l * (16 * L_BLOCKS // RING) + 16 * (i // RING + 1))
                split_used(act, l, f, h)
                raw, hi, _ = half_parts(h)
                nc.scalar.activation(hi, raw(i % RING), ACT.Copy).then_inc(w_hi_done, 1)

            def ffn(l, f):
                for h in range(UP_HALVES):
                    if h % 2 == 0:
                        b = filled(act, l, "layer", "up", f, h // 2, 0)
                        nc.scalar.activation(sg[:, (h // 2) % 2, :], banks[:, b, :], ACT.Silu)\
                            .then_inc(free[b], 1)
                    weights_hi(l, f, h + 2)
                for h in range(UP_HALVES + 2, UP_HALVES + DOWN_HALVES):
                    weights_hi(l, f, h)

            for b in (0, 2):
                act.wait_ge(full[b], 1)
                for k in (2 * b, 2 * b + 1):
                    last = nc.scalar.activation(xs[:, k, :], banks[:, b, (k % 2) * SEQ:(k % 2 + 1) * SEQ],
                                                ACT.Copy)
                last.then_inc(free[b], 1)
                features_hi(b)
            with act.Fori(0, DEPTH) as l:
                for h in range(2):
                    weights_hi(l, 0, h)
                act.wait_ge(sp_abs, l + 1)
                nc.scalar.activation(small[:, 8:16], small[:, 0:8], ACT.Exp).then_inc(sp_exp, 1)
                ffn(l, 0)
                act.wait_ge(lc_done, l + 1)
                turned(l, 0)
                for h in range(HEADS):
                    b = filled(act, l, "layer", "bc", h, 1)
                    nc.scalar.activation(c_sb[:].rearrange("p a b -> p (a b)"), banks[:, b, :], ACT.Copy)\
                        .then_inc(free[b], 1)
                    b = filled(act, l, "layer", "vx", h, 1)
                    act.wait_ge(xc_done, l * HEADS + h + 1)
                    nc.scalar.activation(xr_pad[:, :, 3:3 + SEQ], banks[:, b, :].rearrange("p (a b) -> p a b", a=2),
                                         ACT.Copy).then_inc(free[b], 1)
                for h in range(HEADS):
                    for gate, th in ((0, th_i), (1, th_r)):
                        b = filled(act, l, "layer", "rg", h, gate)
                        for j in range(2):
                            k = 2 * h + j
                            last = nc.scalar.activation(th[:, k, :], banks[:, b, j * SEQ:(j + 1) * SEQ], ACT.Tanh,
                                                        scale=0.5, bias=half_b[:, 8 * gate + k:8 * gate + k + 1])
                        last.then_inc(free[b], 1)
                    nc.scalar.drain()
                    for k in (2 * h, 2 * h + 1):
                        nc.scalar.activation(a_t[:, k, :], th_r[:, k, :], ACT.Exp,
                                             scale=decay[:, k:k + 1], bias=decay[:, k:k + 1])
                    nc.scalar.drain()
                    for k in (2 * h, 2 * h + 1):
                        last = nc.scalar.activation(th_r[:, k, :], th_r[:, k, :], ACT.Tanh,
                                                    scale=decay[:, k:k + 1], bias=decay[:, k:k + 1])
                    last.then_inc(gate_done, 1)
                act.wait_ge(m2_done, l * HEADS + HEADS)
                nc.scalar.activation(th_r[:].rearrange("p a b -> p (a b)"), th_r[:].rearrange("p a b -> p (a b)"),
                                     ACT.Sqrt, scale=-1.0).then_inc(root_done, 1)
                for q in range(6):
                    for side in range(2):
                        b = filled(act, l, "layer", "yg", q, side)
                        k = 4 * (q % 2) + 2 * side
                        if q < 2:
                            last = nc.scalar.activation(gy[:, k:k + 2, :].rearrange("p a b -> p (a b)"), banks[:, b, :],
                                                        ACT.Gelu_apprx_tanh)
                        else:
                            for j in range(2):
                                kk = 8 * (q // 2 - 1) + k + j
                                last = nc.scalar.activation(th_g[:, kk, :], banks[:, b, j * SEQ:(j + 1) * SEQ],
                                                            ACT.Tanh, scale=0.5, bias=half_m[:, kk:kk + 1])
                        last.then_inc(free[b], 1)
                act.wait_ge(m_done, l * 4 + 4)
                for h in range(2):
                    weights_hi(l, 1, h)
                turned(l, 1)
                ffn(l, 1)
                turned(l, 2)

            A = nc.scalar

            def copy(dst, src, then=None, func=ACT.Copy, **kw):
                x = A.activation(dst, src, func, **kw)
                if then is not None:
                    x.then_inc(then, 1)

            act.wait_ge(c_in, 48)
            copy(cond[:].rearrange("p a b -> p (a b)"), c2[:, C2["cond"]:C2["cond"] + 16], S2["cond_done"], ACT.Silu)
            act.wait_ge(xrow_done, 1 + 6 * DEPTH)
            act.wait_ge(S2["ctx_in"], 16)
            for r in range(4):
                copy(f_abs[:, 0, :], xrow[:, r, :], S2["ssq_done"], ACT.Square, accum_out=rs[:, r:r + 1])
                A.drain()

            def modulation(i):
                for u in range(4):
                    b = filled(act, i, "mod", "row", u)
                    copy(mod_rows[:, u * 512:(u + 1) * 512], banks[0:2, b, :], free[b])

            def sine(n):
                act.wait_ge(S2["sin_in"], n + 1)
                copy(z512[0:HY_HIDDEN, n, 0:SEQ], z512[0:HY_HIDDEN, n, SEQ:512], S2["sin_out"], ACT.Sin)

            with act.Fori(0, 2) as i:
                modulation(i)
            sine(0)
            modulation(2)
            sine(1)
            act.wait_ge(S2["gain_done"], 1)

            def pre(seg, layer):
                for k in range(0, KT, 2):
                    b = filled(act, 0, seg, "pre", k)
                    for w in range(2):
                        x = A.activation(xt[:, k, w * SEQ:(w + 1) * SEQ], banks[:, b, w * SEQ:(w + 1) * SEQ],
                                         ACT.Identity, scale=gain[:, layer, k, w:w + 1], bias=mod[:, layer, k, w:w + 1])
                    x.then_inc(free[b], 1)

            pre("even", 0)
            act.wait_ge(S2["abs_in"], 1)
            copy(f_abs[:], f_sum[:], S2["abs_out"], ACT.Abs)
            copy(z[:], f_dif[:], S2["abs_out"], ACT.Abs)
            for p in range(5):
                for h in range(2):
                    b = filled(act, 0, "even", "sp", p, h)
                    copy(spec[:, p, h * 512:(h + 1) * 512], banks[:, b, :], free[b])
            for w in range(2):
                for h in range(2):
                    b = filled(act, 0, "even", "gg", w, h)
                    copy(bcast[:, w, h * 512:(h + 1) * 512], banks[:, b, :], free[b])
            with act.Fori(0, KT) as i:
                act.wait_ge(S2["conv_done"], i + 1)
                for c in range(3):
                    b = filled(act, i, "hyena", "x", c)
                    copy(pad[:, c, :, 1:1 + SEQ], banks[:, b, :].rearrange("p (w n) -> p w n", w=2), free[b])
                b = filled(act, i, "hyena", "g")
                copy(z512[:, 0, :], banks[:, b, :], S2["th_done"], ACT.Tanh, scale=0.5)
                b = filled(act, i, "hyena", "ht")
                copy(hy_gt[:].rearrange("p a b -> p (a b)"), banks[:, b, :], free[b])
            for t in range(2):
                b = filled(act, 0, "kv", "k", t)
                copy(th_a[:, t, :], banks[:, b, :], S2["sq_done"], ACT.Square)
            for t in range(2):
                b = filled(act, 0, "kv", "v", t)
                copy(v_sb[:, 2 * t:2 * t + 2, :].rearrange("p a b -> p (a b)"), banks[:, b, :], free[b])
            for t in range(2):
                b = filled(act, 0, "kv", "kss", t)
                act.wait_ge(S2["row_ok"], t + 1)
                copy(banks[:, b, :], banks[:, b, :], S2["root2"], ACT.Sqrt, scale=1.0)
            for i in range(Q_HEADS // 2):
                for a in range(2):
                    b = filled(act, i, "heads", "q", a)
                    A.drain()
                    qn = c2[:, C2["qk"]:C2["qk"] + 1]
                    copy(q_sb[:, a, :], banks[:, b, :], None, ACT.Copy, scale=qn)
                    if a == 1:
                        filled(act, i, "heads", "qs", 0)
                    copy(tmp_a[:, 0:2, :].rearrange("p a b -> p (a b)"), banks[:, b, :], None, ACT.Square)
                    A.drain().then_inc(S2["qg_done"], 1)
                    for r in range(4):
                        act.wait_ge(S2["p_done"], 8 * i + 4 * a + r + 1)
                        b = plan["heads"]["s", a, r][0]
                        n = ROWS if r < RT else SEQ
                        if r >= 2:
                            filled(act, i, "heads", "pt", a, 1)
                        copy(p_sb[:, r % 2, 0:n], banks[:, b, 0:n], free[b], ACT.Exp, scale=rs[:, 4 + r:5 + r],
                             bias=rs[:, 8 + r:9 + r], accum_out=rs[:, 12 + r:13 + r])
                        if r % 2:
                            for j in ((0, 1) if r == 1 else (2,)):
                                bb = filled(act, i, "heads", "pt", a, j)
                                copy(pt_sb[:, 2 * j:2 * j + 2, :].rearrange("p a b -> p (a b)"), banks[:, bb, :],
                                     free[bb])
                    if i > 0:
                        released(act, i - 1, "heads", "o", a)
                    b = filled(act, i, "heads", "g", a)
                    copy(th_a[:, a, :], banks[:, b, :], S2["th_done"], ACT.Tanh, scale=0.5)

            def post(seg, tiles, key, layer):
                for r in range(tiles):
                    for h in range(2):
                        b = filled(act, 0, seg, "y", *key(h, r))
                        copy(q_j, banks[:, b, :], S2["post_ss"], ACT.Square, accum_out=rs[:, 16 + 2 * r + h:17 + 2 * r + h])
                        A.drain()

            q_j = z512[:, 2, :]
            A.drain()
            act.wait_ge(S2["mix_done"], KT + Q_HEADS)
            post("even_y", 4, lambda h, r: (h, r), 0)
            for r in range(4):
                act.wait_ge(S2["post_done"], 2 * r + 2)
                copy(z[:, 1, :], xrow[:, r, :], S2["ssq_done"], ACT.Square, accum_out=rs[:, r:r + 1])
                A.drain()
            pre("odd", 1)
            for h in range(2):
                b = filled(act, 0, "odd", "gg", h)
                copy(bcast[:, 0, h * 512:(h + 1) * 512], banks[:, b, :], free[b])
            act.wait_ge(S2["gate_ab"], 1)
            copy(g_u[0:64, :], g_t[0:64, :], S2["gate_exp"], ACT.Exp)
            act.wait_ge(S2["gate_ab"], 2)
            copy(g_u[0:64, 0:SEQ], g_u[0:64, SEQ:ROWS], S2["em_in"], ACT.Exp, scale=-1.0)
            b = filled(act, 0, "odd", "ct")
            copy(c_t[:].rearrange("p a b -> p (a b)"), banks[:, b, 0:256], free[b])
            b = filled(act, 0, "odd", "em")
            copy(em_t[:].rearrange("p a b -> p (a b)"), banks[:, b, 0:128], free[b])
            with act.Fori(0, ML_HEADS) as i:
                b = filled(act, i, "ml", "q")
                act.wait_ge(S2["qk_conv"], i + 1)
                copy(q_pad[:, 1:1 + SEQ], banks[:, b, 0:SEQ], free[b])
                b = filled(act, i, "ml", "k")
                copy(k_pad[:, :, 1:1 + SEQ], banks[:, b, :].rearrange("p (w n) -> p w n", w=2), free[b])
                for t in range(2):
                    b = filled(act, i, "ml", "v", t)
                    copy(v_ml[:, 2 * t:2 * t + 2, 0:ML_V], banks[:, b, :].rearrange("p (w n) -> p w n", w=2), free[b])
                act.wait_ge(S2["copied"], i + 1)
                copy(z512[:, 0, 0:SEQ], q_ml[:], None, ACT.Tanh, scale=0.5)
                copy(z512[:, 1, :], k_ml[:], S2["qk_th"], ACT.Tanh, scale=0.5)
                b = filled(act, i, "ml", "o")
                copy(o_ml[:].rearrange("p a b -> p (a b)"), banks[:, b, :], free[b], ACT.Tanh, scale=0.5)
                b = filled(act, i, "ml", "z")
                copy(z_ml[:].rearrange("p a b -> p (a b)"), banks[:, b, :], S2["ml_th"], ACT.Tanh, scale=0.5)
                b = filled(act, i, "ml", "mb")
                act.wait_ge(S2["dm_done"], i + 1)
                for d in range(2):
                    mb = banks[:, b, d * SEQ:(d + 1) * SEQ]
                    for kt in range(2):
                        copy(dec[:, d, kt, :], mb, None, ACT.Exp, scale=-1.0, bias=ml_c[:, MLC + 4 * d + kt:MLC + 4 * d + kt + 1])
                    kt, r = (0, 1) if d == 0 else (1, 0)
                    copy(dec[:, d, 2 + kt, r * P:(r + 1) * P], banks[:, b, d * SEQ + r * P:d * SEQ + (r + 1) * P], None,
                         ACT.Exp, scale=-1.0, bias=ml_c[:, MLC + 4 * d + 2 + kt:MLC + 4 * d + 3 + kt])
                for d in range(2):
                    for r in range(2):
                        x = A.activation(dec[:, d, 2 + r, r * P:(r + 1) * P], dmask[:, d, r * P:(r + 1) * P], ACT.Exp,
                                         scale=-1.0, bias=ml_c[:, MLC + 4 * d + 2 + r:MLC + 4 * d + 3 + r])
                    A.drain().then_inc(S2["dec_done"], 1)
                for d in range(2):
                    for r in range(RT):
                        b = filled(act, i, "ml", "n", d, r)
                        copy(den[:, 2 * d + r:2 * d + r + 1], banks[:, b, ML_V:ML_V + 1], S2["den_in"])
                act.wait_ge(S2["ml_ss_in"], i + 1)
                for r in range(RT):
                    copy(p_ml[:, 0, 0, :], h_ml[:, r, :], S2["ml_ss"], ACT.Square, accum_out=den[:, 16 + r:17 + r])
                    A.drain()
            act.wait_ge(S2["t_done"], 2 * ML_HEADS)
            post("odd_y", RT, lambda h, r: (r, h), 1)

        @block.vector
        def _(dve):
            v = nc.vector

            def turned(l, n):
                for b in (1, 3):
                    filled(dve, l, "layer", "turn", n, b)
                    for k in (2 * b, 2 * b + 1):
                        g0 = LCOL["ln_g"] + 8 * n + k
                        b0 = LCOL["ln_b"] + 8 * n + k
                        last = v.tensor_scalar(xs[:, k, :], banks[:, b, (k % 2) * SEQ:(k % 2 + 1) * SEQ],
                                               lc[:, g0:g0 + 1], lc[:, b0:b0 + 1], ALU.mult,
                                               ALU.add)
                    last.then_inc(free[b], 1)
                if n:
                    features_split(l, n)

            def features_lo(b):
                return v.tensor_tensor(x_lo[:, 2 * b:2 * b + 2, :], xs[:, 2 * b:2 * b + 2, :],
                                       x_hi[:, 2 * b:2 * b + 2, :].bitcast(F32), ALU.subtract)

            def features_split(l, n):
                v.drain()
                for b in (1, 3):
                    v.tensor_copy(x_hi[:, 2 * b:2 * b + 2, :], xs[:, 2 * b:2 * b + 2, :])
                v.drain()
                for b in (1, 3):
                    features_lo(b)
                for j, b in enumerate((0, 2)):
                    dve.wait_ge(x_hi_done, (j + 1) if n is None else l * 4 + (2 * n + j + 1))
                    last = features_lo(b)
                last.then_inc(x_split, 1)

            def weights_lo(l, f, h):
                dve.wait_ge(w_hi_done, halves_before(l, f, h) + 1)
                split_used(dve, l, f, h)
                raw, hi, lo = half_parts(h)
                v.tensor_tensor(lo, raw((AT_FFN[f] + h // 2) % RING), hi.bitcast(F32), ALU.subtract)\
                    .then_inc(w_lo_done, 1)

            def rsqrt(dst, var, tmp):
                v.tensor_scalar(dst.bitcast(I32), var.bitcast(I32), -0.5, float(0x5F3759DF), ALU.mult, ALU.add)
                for _ in range(3):
                    v.drain()
                    v.tensor_tensor(tmp, dst, dst, ALU.mult)
                    v.drain()
                    v.tensor_tensor(tmp, tmp, var, ALU.mult)
                    v.drain()
                    v.tensor_scalar(tmp, tmp, -0.5, 1.5, ALU.mult, ALU.add)
                    v.drain()
                    v.tensor_tensor(dst, dst, tmp, ALU.mult)
                v.drain()

            def norm(l, n, alpha, eps):
                for r in range(RT):
                    filled(dve, l, "layer", "y", n, r)
                    dve.wait_ge(xrow_done, l * 6 + RT * n + 1)
                    v.scalar_tensor_tensor(z[:, r, :], xrow[:, r, :], alpha, yacc[:, r, :], ALU.mult,
                                           ALU.add).then_inc(free[4 + 2 * r], 1)
                    v.drain()
                    for half in range(2):
                        v.bn_stats(stats[:, r, half, :], z[:, r, half * 512:(half + 1) * 512])
                    v.drain()
                    v.bn_aggr(mv[:, r, :], stats[:, r].rearrange("p a b -> p (a b)"))
                    v.drain()
                    v.tensor_scalar(rstd[:, r, 0:1], mv[:, r, 1:2], eps, None, ALU.add)
                    v.drain()
                    rsqrt(rstd[:, r, 1:2], rstd[:, r, 0:1], rstd[:, r, 2:3])
                    v.tensor_scalar(z[:, r, :], z[:, r, :], mv[:, r, 0:1], rstd[:, r, 1:2], ALU.subtract,
                                    ALU.mult).then_inc(norm_done, 1)

            def ffn(l, f):
                for j in range(FJ):
                    weights_lo(l, f, 2 * j + 2)
                    b = filled(dve, l, "layer", "up", f, j, 1)
                    released(dve, l, "layer", "up", f, j, 0)
                    s, hi, lo = sg[:, j % 2, :], *(g[:, 2 * j:2 * j + 2, :].rearrange("p a b -> p (a b)")
                                                   for g in (gt_hi, gt_lo))
                    v.scalar_tensor_tensor(s, banks[:, b, :], 0.5, s, ALU.mult, ALU.mult)
                    v.drain()
                    v.tensor_copy(hi, s)
                    v.drain()
                    v.tensor_tensor(lo, s, hi.bitcast(F32), ALU.subtract).then_inc(free[b], 1)
                    weights_lo(l, f, 2 * j + 3)
                for h in range(UP_HALVES + 2, UP_HALVES + DOWN_HALVES):
                    weights_lo(l, f, h)

            def log1p(dst, y, tmp, tmp2):
                v.tensor_scalar(tmp, y, 2.0, None, ALU.add)
                v.drain()
                v.reciprocal(tmp, tmp)
                v.drain()
                v.tensor_tensor(tmp, tmp, y, ALU.mult)
                v.drain()
                v.tensor_tensor(tmp2, tmp, tmp, ALU.mult)
                v.drain()
                v.tensor_scalar(dst, tmp2, 2.0 / 17.0, 2.0 / 15.0, ALU.mult, ALU.add)
                for odd in (13.0, 11.0, 9.0, 7.0, 5.0, 3.0, 1.0):
                    v.drain()
                    v.tensor_tensor(dst, dst, tmp2, ALU.mult)
                    v.drain()
                    v.tensor_scalar(dst, dst, 2.0 / odd, None, ALU.add)
                v.drain()
                v.tensor_tensor(dst, dst, tmp, ALU.mult)
                v.drain()

            dve.sem_inc(xc_done, 1)
            dve.wait_ge(c_in, 48)
            for b in (1, 3):
                dve.wait_ge(full[b], 1)
                for k in (2 * b, 2 * b + 1):
                    last = v.tensor_copy(xs[:, k, :], banks[:, b, (k % 2) * SEQ:(k % 2 + 1) * SEQ])
                last.then_inc(free[b], 1)
            features_split(0, None)
            dve.wait_ge(ready, 2)
            with dve.Fori(0, DEPTH) as l:
                for h in range(2):
                    weights_lo(l, 0, h)
                v.drain()
                for b in (0, 2):
                    dve.wait_ge(free[b], l * layer_uses + 2)
                v.tensor_copy(lc[:], colsb[:, bass.ds(l * LCOLS, LCOLS)]).then_inc(lc_done, 1)
                v.drain()
                ap = lc[:, LCOL["a_param"]:LCOL["a_param"] + 8]
                v.scalar_tensor_tensor(small[:, 0:8], ap, -1.0, ap, ALU.mult, ALU.min).then_inc(sp_abs, 1)
                v.tensor_scalar(half_b[:], lc[:, LCOL["rg_b"]:LCOL["rg_b"] + 16], 0.5, None, ALU.mult)
                v.tensor_scalar(half_m[:], lc[:, LCOL["b_merge"]:LCOL["b_merge"] + 16], 0.5, None, ALU.mult)
                v.tensor_scalar(small[:, 16:24], ap, -1.0, 0.0, ALU.mult, ALU.max)
                dve.wait_ge(sp_exp, l + 1)
                log1p(small[:, 24:32], small[:, 8:16], small[:, 32:40], small[:, 40:48])
                v.tensor_tensor(small[:, 24:32], small[:, 24:32], small[:, 16:24], ALU.add)
                v.drain()
                v.tensor_scalar(decay[:], small[:, 24:32], -LRU_C / 2, None, ALU.mult)
                ffn(l, 0)
                norm(l, 0, ALPHA, LN_EPS)
                turned(l, 0)

                def taps(name, k, n):
                    return [lc[:, LCOL[name] + 8 * i + k:LCOL[name] + 8 * i + k + 1] for i in range(n)]

                for h in range(HEADS):
                    v.drain()
                    released(dve, l, "layer", "bc", h, 1)
                    b = filled(dve, l, "layer", "vx", h, 0)
                    v.tensor_tensor(cv_pad[:, :, 2:2 + SEQ], c_sb[:], banks[:, b, :].rearrange("p (a b) -> p a b", a=2),
                                    ALU.mult).then_inc(free[b], 1)
                    v.drain()
                    b = filled(dve, l, "layer", "bc", h, 0)
                    w = [taps("sc_w", 2 * h + j, 3) for j in range(2)]
                    for j in range(2):
                        v.tensor_scalar(ctmp[:, j, :], cv_pad[:, j, 0:SEQ], w[j][0], None, ALU.mult)
                    for i in (1, 2):
                        v.drain()
                        for j in range(2):
                            v.scalar_tensor_tensor(ctmp[:, j, :], cv_pad[:, j, i:i + SEQ], w[j][i], ctmp[:, j, :],
                                                   ALU.mult, ALU.add)
                    v.drain()
                    v.tensor_tensor(ut[:, 2 * h:2 * h + 2, :], ctmp[:, 0:2, :],
                                    banks[:, b, :].rearrange("p (a b) -> p a b", a=2), ALU.mult)\
                        .then_inc(free[b], 1)
                    released(dve, l, "layer", "vx", h, 1)
                    w = [taps("rc_w", 2 * h + j, 4) for j in range(2)]
                    for j in range(2):
                        k = 2 * h + j
                        v.tensor_scalar(xct[:, k, :], xr_pad[:, j, 0:SEQ], w[j][0],
                                        lc[:, LCOL["rc_b"] + k:LCOL["rc_b"] + k + 1], ALU.mult, ALU.add)
                    for i in (1, 2, 3):
                        v.drain()
                        for j in range(2):
                            last = v.scalar_tensor_tensor(xct[:, 2 * h + j, :], xr_pad[:, j, i:i + SEQ], w[j][i],
                                                          xct[:, 2 * h + j, :], ALU.mult, ALU.add)
                    last.then_inc(xc_done, 1)
                for h in range(HEADS):
                    dve.wait_ge(gate_done, l * HEADS + h + 1)
                    two = slice(2 * h, 2 * h + 2)
                    v.tensor_tensor(ctmp[:, 0:2, :], a_t[:, two, :], a_t[:, two, :], ALU.mult)
                    v.scalar_tensor_tensor(th_i[:, two, :], th_i[:, two, :], 1.0, xct[:, two, :], ALU.add, ALU.mult)
                    v.drain()
                    v.scalar_tensor_tensor(th_r[:, two, :], ctmp[:, 0:2, :], 1.0, th_r[:, two, :], ALU.add,
                                           ALU.mult).then_inc(m2_done, 1)
                    v.drain()
                dve.wait_ge(root_done, l + 1)
                v.memset(th_r[:, :, 0:1], 1.0)
                v.drain()
                v.scalar_tensor_tensor(th_i[:].rearrange("p a b -> p (a b)"), th_i[:].rearrange("p a b -> p (a b)"),
                                       0.5, th_r[:].rearrange("p a b -> p (a b)"), ALU.mult, ALU.mult)
                v.drain()
                for k in range(KT):
                    v.tensor_tensor_scan(th_r[:, k, :], a_t[:, k, :], th_i[:, k, :], 0.0, ALU.mult, ALU.add)
                v.drain()
                for side in range(2):
                    released(dve, l, "layer", "yg", 1, side)
                v.tensor_tensor(a_t[:].rearrange("p a b -> p (a b)"), th_r[:].rearrange("p a b -> p (a b)"),
                                gy[:].rearrange("p a b -> p (a b)"), ALU.mult).then_inc(hg_done, 1)
                for q in range(2):
                    for side in range(2):
                        b = filled(dve, l, "layer", "oc", q, side)
                        k = 4 * q + 2 * side
                        released(dve, l, "layer", "yg", 2 + q, side)
                        v.scalar_tensor_tensor(mt[:, k:k + 2, :].rearrange("p a b -> p (a b)"),
                                               th_g[:, k:k + 2, :].rearrange("p a b -> p (a b)"), 1.0,
                                               banks[:, b, :], ALU.add, ALU.mult).then_inc(free[b], 1)
                for q in range(2):
                    for side in range(2):
                        b = filled(dve, l, "layer", "or", q, side)
                        k = 4 * q + 2 * side
                        released(dve, l, "layer", "yg", 4 + q, side)
                        v.scalar_tensor_tensor(th_g[:, 8 + k:10 + k, :].rearrange("p a b -> p (a b)"),
                                               th_g[:, 8 + k:10 + k, :].rearrange("p a b -> p (a b)"), 1.0,
                                               banks[:, b, :], ALU.add, ALU.mult).then_inc(free[b], 1)
                        v.drain()
                        v.tensor_tensor(mt[:, k:k + 2, :], mt[:, k:k + 2, :], th_g[:, 8 + k:10 + k, :],
                                        ALU.add).then_inc(m_done, 1)
                for h in range(2):
                    weights_lo(l, 1, h)
                norm(l, 1, 2 * ALPHA, 4 * LN_EPS)
                turned(l, 1)
                ffn(l, 1)
                norm(l, 2, ALPHA, LN_EPS)
                turned(l, 2)

            def flat(t):
                return t.rearrange("p a b -> p (a b)")

            def prenorm(layer, dst):
                dve.wait_ge(S2["ssq_done"], 4 * layer + 4)
                v.tensor_scalar(rs[:, 24:28], rs[:, 0:4], 1.0 / D, NORM_EPS, ALU.mult, ALU.add)
                v.drain()
                rsqrt(rs[:, 28:32], rs[:, 24:28], rs[:, 40:44])
                for r in range(4):
                    v.tensor_scalar(dst[:, r, :], ident, rs[:, 28 + r:29 + r], None, ALU.mult)\
                        .then_inc(S2["zz_done"], 1)

            def modulation(i):
                b = filled(dve, i, "mod", "mod")
                v.tensor_tensor(flat(mod[:].rearrange("p l t w -> p (l t) w"))[:, bass.ds(i * 32, 32)],
                                banks[:, b, 0:32], c2[:, bass.ds(i * 32 + C2["b_mod"], 32)], ALU.add)\
                    .then_inc(free[b], 1)

            def sine_angle(n, key):
                b = filled(dve, 0, "even", key)
                u, w_ = z512[0:HY_HIDDEN, n, SEQ:512], z512[0:HY_HIDDEN, 2 + n, 0:SEQ]
                v.tensor_scalar(u, banks[0:HY_HIDDEN, b, 0:SEQ], hyf[0:HY_HIDDEN, n:n + 1], hyf[0:HY_HIDDEN, 2:3],
                                ALU.add, ALU.mult).then_inc(free[b], 1)
                v.drain()
                v.tensor_scalar(w_, u, 1.0 / TWO_PI, MAGIC, ALU.mult, ALU.add)
                v.drain()
                v.tensor_scalar(w_, w_, MAGIC, None, ALU.subtract)
                for part_ in TWO_PI_PARTS:
                    v.drain()
                    v.scalar_tensor_tensor(u, w_, -part_, u, ALU.mult, ALU.add)
                v.drain()
                v.tensor_scalar(u, u, PI_BELOW, -PI_BELOW, ALU.min, ALU.max).then_inc(S2["sin_in"], 1)

            prenorm(0, diag)
            dve.wait_ge(xrow_done, 1 + 6 * DEPTH)
            with dve.Fori(0, 2) as i:
                modulation(i)
            dve.wait_ge(S2["hy_in"], 48)
            sine_angle(0, "f1")
            modulation(2)
            sine_angle(1, "f2")
            for layer in range(2):
                v.scalar_tensor_tensor(gain[:, layer].rearrange("p k w -> p (k w)"),
                                       mod[:, layer, 8:16, :].rearrange("p k w -> p (k w)"), 1.0,
                                       c2[:, C2["g_pre"] + 16 * layer:C2["g_pre"] + 16 * (layer + 1)], ALU.add, ALU.mult)
                v.tensor_tensor(gcol[:, layer].rearrange("p k w -> p (k w)"),
                                mod[:, layer, 16:24, :].rearrange("p k w -> p (k w)"),
                                c2[:, C2["g_post"] + 16 * layer:C2["g_post"] + 16 * (layer + 1)], ALU.mult)
            v.drain().then_inc(S2["gain_done"], 1)
            for t in range(2):
                for q in range(4):
                    b = filled(dve, 0, "even", "f3", t, q)
                    side, h = q // 2, q % 2
                    dst = (f_sum, f_dif)[side]
                    v.tensor_tensor(dst[:, t, h * 512:(h + 1) * 512], window[:, t, h * 512:(h + 1) * 512], banks[:, b, :],
                                    ALU.mult).then_inc(free[b], 1)

            def pre(seg, layer):
                for k in range(1, KT, 2):
                    b = filled(dve, 0, seg, "pre", k)
                    for w in range(2):
                        x = v.tensor_scalar(xt[:, k, w * SEQ:(w + 1) * SEQ], banks[:, b, w * SEQ:(w + 1) * SEQ],
                                            gain[:, layer, k, w:w + 1], mod[:, layer, k, w:w + 1], ALU.mult, ALU.add)
                    x.then_inc(free[b], 1)

            pre("even", 0)
            v.drain()
            v.memset(f_dif[0:1, 0, :], 0.0)
            v.drain()
            v.tensor_tensor(flat(f_abs[:]), flat(f_sum[:]), flat(f_dif[:]), ALU.add)
            v.tensor_tensor(flat(z[:]), flat(f_sum[:]), flat(f_dif[:]), ALU.subtract)
            v.drain()
            v.tensor_copy(flat(f_sum[:]), flat(f_abs[:]))
            v.tensor_copy(flat(f_dif[:]), flat(z[:]))
            v.drain().then_inc(S2["abs_in"], 1)
            dve.wait_ge(S2["abs_out"], 2)
            v.tensor_tensor(flat(f_abs[:]), flat(f_abs[:]), flat(z[:]), ALU.max).then_inc(S2["f_done"], 1)
            v.drain()
            for w in range(2):
                for k in range(KT):
                    v.tensor_scalar(z[:, w, k * P:(k + 1) * P], ident, gcol[:, 0, k, w:w + 1], None, ALU.mult)
            v.drain().then_inc(S2["diag_done"], 1)
            b = filled(dve, 0, "even", "fn")
            v.reciprocal(rs[:, 32:40], banks[:, b, 0:8]).then_inc(free[b], 1)

            for p in (3, 4):
                for h in range(2):
                    released(dve, 0, "even", "sp", p, h)
            v.memset(spec[0:1, 3, :], 0.0)
            for w in range(2):
                for h in range(2):
                    released(dve, 0, "even", "gg", w, h)
            v.drain()
            v.memset(pad[:, :, :, 0:1], 0.0)
            v.memset(pad[:, :, :, SEQ + 1:SEQ + 2], 0.0)
            v.drain().then_inc(S2["conv_done"], 1)
            with dve.Fori(0, KT) as i:
                v.tensor_copy(hyc[:, 0:HYC], c2[:, bass.ds(i * HYC + C2["hy"], HYC)])
                v.tensor_copy(hyc[:, HYC:HYC + 1], rs[:, bass.ds(i + 32, 1)])
                v.drain()
                for c in range(3):
                    released(dve, i, "hyena", "x", c)
                    v.tensor_scalar(conved[:, c, :].rearrange("p (w n) -> p w n", w=2), pad[:, c, :, 0:SEQ],
                                    hyc[:, 3 * c:3 * c + 1], hyc[:, 9 + c:10 + c], ALU.mult, ALU.add)
                for j in (1, 2):
                    v.drain()
                    for c in range(3):
                        o = conved[:, c, :].rearrange("p (w n) -> p w n", w=2)
                        v.scalar_tensor_tensor(o, pad[:, c, :, j:j + SEQ], hyc[:, 3 * c + j:3 * c + j + 1], o, ALU.mult,
                                               ALU.add)
                v.drain().then_inc(S2["conv_done"], 1)
                v.tensor_tensor(hy_g[:], conved[:, 1, :], conved[:, 2, :], ALU.mult).then_inc(S2["hg_in"], 1)
                b = filled(dve, i, "hyena", "g")
                dve.wait_ge(S2["th_done"], i + 1)
                v.scalar_tensor_tensor(z512[:, 1, :], z512[:, 0, :], 1.0, banks[:, b, :], ALU.add, ALU.mult)\
                    .then_inc(free[b], 1)
                v.drain()
                v.tensor_tensor(z512[:, 1, :], z512[:, 1, :], conved[:, 0, :], ALU.mult)
                br = filled(dve, i, "hyena", "ur")
                bi = filled(dve, i, "hyena", "ui")
                ur = banks[:, br, :].rearrange("p (k w n) -> p k w n", k=2, w=2)
                ui = banks[:, bi, :].rearrange("p (k w n) -> p k w n", k=2, w=2)
                cs = bass.ds(i * P, P)
                t4 = z512[:, 2:4, :].rearrange("p c (k w n) -> p c k w n", k=2, w=2)
                for w in range(2):
                    v.tensor_tensor(prod[:, 0, :, w, :], ur[:, :, w, :], spec[:, 0:3:2, cs], ALU.mult)
                    x = v.tensor_tensor(prod[:, 1, :, w, :], ur[:, :, w, :], spec[:, 3:5, cs], ALU.mult)
                x.then_inc(free[br], 1)
                for w in range(2):
                    v.tensor_tensor(t4[:, 0, :, w, :], ui[:, :, w, :], spec[:, 3:5, cs], ALU.mult)
                    x = v.tensor_tensor(t4[:, 1, :, w, :], ui[:, :, w, :], spec[:, 1:3, cs], ALU.mult)
                x.then_inc(free[bi], 1)
                v.drain()
                pr = prod[:].rearrange("p c k w n -> p c (k w n)")
                v.tensor_tensor(pr[:, 0, :], pr[:, 0, :], z512[:, 2, :], ALU.subtract)
                v.tensor_tensor(pr[:, 1, :], pr[:, 1, :], z512[:, 3, :], ALU.add)
                v.drain().then_inc(S2["prod_done"], 1)
                v.tensor_scalar(z512[:, 2, :], hy_g[:], hyc[:, 12:13], None, ALU.mult)
                v.drain()
                b = filled(dve, i, "hyena", "hc")
                v.scalar_tensor_tensor(z512[:, 2, :], banks[:, b, :], hyc[:, 13:14], z512[:, 2, :], ALU.mult,
                                       ALU.add).then_inc(free[b], 1)
                v.drain()
                v.tensor_tensor(flat(mixt[:])[:, bass.ds(i * ROWS, ROWS)], z512[:, 2, :], z512[:, 1, :], ALU.mult)\
                    .then_inc(S2["mix_done"], 1)
                v.drain()

            def rope(dst, src, b, tmp):
                v.tensor_tensor(tmp[:, 0, :], src, cos, ALU.mult)
                v.tensor_tensor(tmp[:, 1, :], sin, banks[:, b, 0:SEQ], ALU.mult)
                v.drain()
                return v.tensor_tensor(dst, tmp[:, 0, :], tmp[:, 1, :], ALU.add)

            kn = c2[:, C2["qk"] + 1:C2["qk"] + 2]
            for t in range(2):
                b = filled(dve, 0, "kv", "kss", t)
                v.tensor_scalar(banks[:, b, :], banks[:, b, :], 1.0 / HD, NORM_EPS, ALU.mult, ALU.add)\
                    .then_inc(S2["row_ok"], 1)
            for t in range(2):
                dve.wait_ge(S2["root2"], t + 1)
                b = plan["kv"]["kss", t][0]
                v.reciprocal(tmp_a[:, 0:2, :].rearrange("p a b -> p (a b)"), banks[:, b, :]).then_inc(free[b], 1)
                v.drain()
                b = filled(dve, 0, "kv", "k", t)
                v.scalar_tensor_tensor(k_t[:, t, :], banks[:, b, :], kn, tmp_a[:, 0:2, :].rearrange("p a b -> p (a b)"),
                                       ALU.mult, ALU.mult).then_inc(free[b], 1)
                v.drain().then_inc(S2["kn_done"], 1)
            for t in range(2):
                b = filled(dve, 0, "kv", "kr", t)
                rope(k_t[:, t, 0:SEQ], k_t[:, t, 0:SEQ], b, tmp_a)
                v.drain().then_inc(S2["k_done"], 1)
                dve.sem_inc(free[b], 1)
            for i in range(Q_HEADS // 2):
                for a in range(2):
                    b = filled(dve, i, "heads", "qs", a)
                    v.tensor_scalar(rs[:, 24:28], banks[:, b, 0:4], HD * NORM_EPS, None, ALU.add).then_inc(free[b], 1)
                    v.drain()
                    rsqrt(rs[:, 4:8], rs[:, 24:28], rs[:, 28:32])
                    b = filled(dve, i, "heads", "qr", a)
                    rope(q_sb[:, a, 0:SEQ], q_sb[:, a, 0:SEQ], b, tmp_a[:, 2:4, :])
                    v.drain().then_inc(S2["rope_done"], 1)
                    dve.sem_inc(free[b], 1)
                    dve.wait_ge(S2["qg_done"], 2 * i + a + 1)
                    dve.sem_inc(free[plan["heads"]["q", a][0]], 1)
                    for r in range(4):
                        b = filled(dve, i, "heads", "s", a, r)
                        n = ROWS if r < RT else SEQ
                        v.reduce_max(rs[:, 40:41], banks[:, b, 0:n], axis=mybir.AxisListType.X)
                        v.drain()
                        v.scalar_tensor_tensor(rs[:, 8 + r:9 + r], rs[:, 40:41], -1.0, rs[:, 4 + r:5 + r], ALU.mult,
                                               ALU.mult)
                        v.drain().then_inc(S2["p_done"], 1)
                        released(dve, i, "heads", "s", a, r)
                        v.reciprocal(rs[:, 41:42], rs[:, 12 + r:13 + r])
                        v.drain()
                        v.tensor_scalar(p_sb[:, r % 2, 0:n], p_sb[:, r % 2, 0:n], rs[:, 41:42], None, ALU.mult)
                        v.drain().then_inc(S2["pn_done"], 1)
                    b = filled(dve, i, "heads", "g", a)
                    dve.wait_ge(S2["th_done"], KT + 2 * i + a + 1)
                    v.scalar_tensor_tensor(th_a[:, a, :], th_a[:, a, :], 1.0, banks[:, b, :], ALU.add, ALU.mult)\
                        .then_inc(free[b], 1)
                    v.drain()
                    b = filled(dve, i, "heads", "o", a)
                    v.tensor_tensor(mixt[:, KT + 2 * i + a, :], th_a[:, a, :], banks[:, b, :], ALU.mult)\
                        .then_inc(free[b], 1)
                    v.drain().then_inc(S2["mix_done"], 1)

            def post(seg, tiles, key, layer, done):
                for r in range(tiles):
                    w = r // RT
                    dve.wait_ge(S2["post_ss"], 8 * layer + 2 * r + 2)
                    v.tensor_tensor(rs[:, 24:25], rs[:, 16 + 2 * r:17 + 2 * r], rs[:, 17 + 2 * r:18 + 2 * r], ALU.add)
                    v.drain()
                    v.tensor_scalar(rs[:, 24:25], rs[:, 24:25], 1.0 / D, 4 * NORM_EPS, ALU.mult, ALU.add)
                    v.drain()
                    rsqrt(rs[:, 25:26], rs[:, 24:25], rs[:, 26:27])
                    for h in range(2):
                        b = plan[seg]["y", *key(h, r)][0]
                        v.scalar_tensor_tensor(z512[:, h, :], banks[:, b, :], rs[:, 25:26],
                                               bcast[:, w, h * 512:(h + 1) * 512], ALU.mult, ALU.mult)\
                            .then_inc(free[b], 1)
                        v.drain()
                        v.tensor_tensor(xrow[:, r, h * 512:(h + 1) * 512], xrow[:, r, h * 512:(h + 1) * 512],
                                        z512[:, h, :], ALU.add).then_inc(S2["post_done"], 1)
                        v.drain()

            post("even_y", 4, lambda h, r: (h, r), 0, 8)
            prenorm(1, diag2)
            pre("odd", 1)
            for k in range(KT):
                v.tensor_scalar(z[:, 0, k * P:(k + 1) * P], ident, gcol[:, 1, k, 0:1], None, ALU.mult)
            v.drain().then_inc(S2["diag_done"], 1)
            gb = c2[0:64, C2["gate_b"]:C2["gate_b"] + 2]
            b = filled(dve, 0, "odd", "gf")
            for p0, p1, c0 in ((0, 32, SEQ), (32, 64, 0)):
                for j in range(2):
                    v.tensor_scalar(g_b[p0:p1, j * SEQ:(j + 1) * SEQ], banks[p0:p1, b, (c0 + j * SEQ) % ROWS:(c0 + j * SEQ) % ROWS + SEQ],
                                    gb[p0:p1, 1:2], None, ALU.add)
            v.drain()
            dve.sem_inc(free[b], 1)
            b = filled(dve, 0, "odd", "gi")
            for p0, p1, c0 in ((0, 32, SEQ), (32, 64, 0)):
                for j in range(2):
                    v.tensor_scalar(g_i[p0:p1, j * SEQ:(j + 1) * SEQ], banks[p0:p1, b, (c0 + j * SEQ) % ROWS:(c0 + j * SEQ) % ROWS + SEQ],
                                    gb[p0:p1, 0:1], None, ALU.add)
            v.drain()
            dve.sem_inc(free[b], 1)
            G = slice(0, 64)
            v.scalar_tensor_tensor(g_t[G, :], g_b[G, :], -1.0, g_b[G, :], ALU.mult, ALU.min)
            v.drain().then_inc(S2["gate_ab"], 1)
            dve.wait_ge(S2["gate_exp"], 1)
            log1p(g_c[G, :], g_u[G, :], g_t[G, :], g_m[G, :])
            v.scalar_tensor_tensor(g_b[G, :], g_b[G, :], 0.0, g_c[G, :], ALU.min, ALU.subtract)
            v.memset(g_t[G, :], 1.0)
            v.drain()
            v.tensor_tensor_scan(g_m[0:32, :], g_t[0:32, :], g_b[0:32, :], 0.0, ALU.mult, ALU.add)
            v.drain()
            v.tensor_tensor_scan(g_m[32:64, ::-1], g_t[32:64, ::-1], g_b[32:64, ::-1], 0.0, ALU.mult, ALU.add)
            v.drain()
            v.tensor_copy(g_b[G, :], g_m[G, :])
            v.drain()
            v.tensor_tensor(g_c[G, :], g_i[G, :], g_b[G, :], ALU.subtract)
            v.drain().then_inc(S2["ct_in"], 1)
            v.tensor_tensor_scan(g_m[0:32, :], g_c[0:32, :], g_c[0:32, :], 0.0, ALU.max, ALU.max)
            v.drain()
            v.tensor_tensor_scan(g_m[32:64, ::-1], g_c[32:64, ::-1], g_c[32:64, ::-1], 0.0, ALU.max, ALU.max)
            v.drain()
            for p0, p1, c0 in ((0, 32, SEQ), (32, 64, 0)):
                v.tensor_tensor(g_u[p0:p1, SEQ:ROWS], g_b[p0:p1, c0:c0 + SEQ], g_m[p0:p1, c0:c0 + SEQ], ALU.add)
                v.drain()
            v.drain().then_inc(S2["gate_ab"], 1)
            for t in (q_pad[:, 0:1], q_pad[:, SEQ + 1:SEQ + 2], k_pad[:, :, 0:1], k_pad[:, :, SEQ + 1:SEQ + 2]):
                v.memset(t, 0.0)
            v.memset(v_ml[:, :, ML_V:ML_V + 1], 1.0)
            v.memset(dec[:].rearrange("p d k t -> p (d k t)"), 0.0)
            v.drain().then_inc(S2["qk_conv"], 1)
            released(dve, 0, "odd", "ct")
            released(dve, 0, "odd", "em")
            c4 = c_t[:].rearrange("p k (d h) -> p d k h", d=2)
            e4 = em_t[:].rearrange("p r (d h) -> p d r h", d=2)
            with dve.Fori(0, ML_HEADS) as i:
                v.tensor_copy(ml_c[:, 0:MLC], c2[:, bass.ds(i * MLC + C2["ml"], MLC)])
                mc = ml_c[:, MLC:MLC + 8].rearrange("p (d k) -> p d k", d=2)
                v.tensor_copy(mc[:, 0, :], c4[:, 0, :, bass.ds(i, 1)].squeeze(2))
                v.tensor_copy(mc[:, 1, 0:2], c4[:, 1, 2:4, bass.ds(i, 1)].squeeze(2))
                v.tensor_copy(mc[:, 1, 2:4], c4[:, 1, 0:2, bass.ds(i, 1)].squeeze(2))
                v.tensor_copy(ml_c[:, MLC + 8:MLC + 12].rearrange("p (d r) -> p d r", d=2),
                              e4[:, :, :, bass.ds(i, 1)].squeeze(3))
                v.drain().then_inc(S2["hc_done"], 1)
                released(dve, i, "ml", "q")
                released(dve, i, "ml", "k")
                v.tensor_scalar(q_ml[:], q_pad[:, 0:SEQ], ml_c[:, 0:1], ml_c[:, 3:4], ALU.mult, ALU.add)
                k2 = k_ml[:].rearrange("p (w n) -> p w n", w=2)
                v.tensor_scalar(k2, k_pad[:, :, 0:SEQ], ml_c[:, 4:5], ml_c[:, 7:8], ALU.mult, ALU.add)
                for j in (1, 2):
                    v.drain()
                    v.scalar_tensor_tensor(q_ml[:], q_pad[:, j:j + SEQ], ml_c[:, j:j + 1], q_ml[:], ALU.mult, ALU.add)
                    v.scalar_tensor_tensor(k2, k_pad[:, :, j:j + SEQ], ml_c[:, 4 + j:5 + j], k2, ALU.mult, ALU.add)
                v.drain().then_inc(S2["qk_conv"], 1)
                dve.sem_inc(S2["copied"], 1)
                dve.wait_ge(S2["qk_th"], i + 1)
                v.scalar_tensor_tensor(q_ml[:], z512[:, 0, 0:SEQ], 1.0, q_ml[:], ALU.add, ALU.mult)
                v.scalar_tensor_tensor(k_ml[:], z512[:, 1, :], 1.0, k_ml[:], ALU.add, ALU.mult)
                v.drain().then_inc(S2["qk_done"], 1)
                dve.wait_ge(S2["ml_th"], i + 1)
                b = plan["ml"]["z",][0]
                v.scalar_tensor_tensor(flat(z_ml[:]), flat(z_ml[:]), 1.0, banks[:, b, :], ALU.add, ALU.mult)\
                    .then_inc(free[b], 1)
                b = filled(dve, i, "ml", "mb")
                mb = banks[:, b, :].rearrange("p (d r n) -> p d r n", d=2, r=2)
                for d in range(2):
                    for r in range(2):
                        v.tensor_tensor(dmask[:, d, r * P:(r + 1) * P], mask[:, d, :], mb[:, d, r, :], ALU.add)
                v.drain().then_inc(S2["dm_done"], 1)
                bs = [filled(dve, i, "ml", "s", half) for half in range(2)]
                for d in range(2):
                    dve.wait_ge(S2["dec_done"], i * 2 + d + 1)
                    for half in range(2):
                        x = v.scalar_tensor_tensor(p_ml[:, d, 2 * half:2 * half + 2, :].rearrange("p k t -> p (k t)"),
                                                   banks[:, bs[half], :], 0.25 * HD ** -0.5,
                                                   dec[:, d, 2 * half:2 * half + 2, :].rearrange("p k t -> p (k t)"),
                                                   ALU.mult, ALU.mult)
                        x.then_inc(S2["pml_done"], 1)
                v.drain()
                for bb in (plan["ml"]["mb",][0], *bs):
                    dve.sem_inc(free[bb], 1)
                dve.wait_ge(S2["den_in"], i * 4 + 4)
                v.scalar_tensor_tensor(den[:, 4:8], den[:, 0:4], -1.0, den[:, 0:4], ALU.mult, ALU.max)
                v.drain()
                v.tensor_tensor(den[:, 4:8], den[:, 4:8], ml_c[:, MLC + 8:MLC + 12], ALU.max)
                v.drain()
                v.reciprocal(den[:, 8:12], den[:, 4:8])
                v.drain()
                for r in range(RT):
                    b = plan["ml"]["n", 0, r][0]
                    v.tensor_scalar(h_ml[:, r, :], banks[:, b, 0:ML_V], den[:, 8 + r:9 + r], None, ALU.mult)\
                        .then_inc(free[b], 1)
                v.drain()
                for r in range(RT):
                    b = plan["ml"]["n", 1, r][0]
                    v.scalar_tensor_tensor(h_ml[:, r, :], banks[:, b, 0:ML_V], den[:, 10 + r:11 + r], h_ml[:, r, :],
                                           ALU.mult, ALU.add).then_inc(free[b], 1)
                v.drain()
                v.scalar_tensor_tensor(flat(h_ml[:]), flat(o_ml[:]), 1.0, flat(h_ml[:]), ALU.add, ALU.mult)
                v.drain().then_inc(S2["ml_ss_in"], 1)
                dve.wait_ge(S2["ml_ss"], i * 2 + 2)
                v.tensor_scalar(den[:, 20:22], den[:, 16:18], 1.0 / ML_V, 4 * NORM_EPS, ALU.mult, ALU.add)
                v.drain()
                rsqrt(den[:, 22:24], den[:, 20:22], den[:, 24:26])
                for r in range(RT):
                    v.tensor_scalar(h_ml[:, r, :], h_ml[:, r, :], den[:, 22 + r:23 + r], None, ALU.mult)\
                        .then_inc(S2["hn_done"], 1)
                v.drain()
                b = filled(dve, i, "ml", "t")
                for t in range(2):
                    v.scalar_tensor_tensor(flat(mt2)[:, bass.ds(i * 2 * SEQ + t * SEQ, SEQ)],
                                           banks[:, b, t * SEQ:(t + 1) * SEQ], ml_c[:, 8 + t:9 + t], z_ml[:, t, :],
                                           ALU.mult, ALU.mult).then_inc(S2["t_done"], 1)
                v.drain()
                dve.sem_inc(free[b], 1)
            post("odd_y", RT, lambda h, r: (r, h), 1, 4)


def weight_blocks(i):
    def block(m):
        k, n = m.shape
        assert (k, n) == (D, 512), (k, n)
        return m.reshape(KT, P, n).transpose(1, 0, 2).reshape(P, BLK)

    def units(m):
        k = m.shape[0] // P
        u = [m[j * P:(j + 1) * P, h * 512:(h + 1) * 512] for h in range(2) for j in range(k)]
        u += [np.zeros_like(u[0])] * (-len(u) % KT)
        return [np.stack(u[j:j + KT], 1).reshape(P, BLK) for j in range(0, len(u), KT)]

    out = []
    for l in range(DEPTH):
        def ffn(f):
            w1 = i["ffn_w1"][l, f]
            for j in range(FJ):
                c = 256 * j
                out.append(block(np.concatenate([w1[:, c:c + 256], w1[:, D_FF + c:D_FF + c + 256]], 1)))
            out.extend(units(i["ffn_w2"][l, f]))

        ffn(0)
        w = i["w_in"][l]
        for h in range(HEADS):
            for a, b in ((0, 1), (2, 3)):
                out.append(block(np.concatenate([w[:, a * D + 256 * h:a * D + 256 * h + 256],
                                                 w[:, b * D + 256 * h:b * D + 256 * h + 256]], 1)))
        for g in range(2):
            m = i["rg_w"][l, g].reshape(HEADS * 2, P, 256).transpose(1, 0, 2).reshape(P, 2048)
            out.append(np.concatenate([m, np.zeros_like(m)], 1))
        for q in range(6):
            out.append(block(w[:, 4 * D + 512 * q:4 * D + 512 * (q + 1)]))
        for m in (i["w_out_conv"][l], i["w_out_rnn"][l]):
            for q in range(2):
                out.append(block(m[:, 512 * q:512 * (q + 1)]))
        out.extend(units(i["w_o"][l]))
        ffn(1)
    return out


def second_blocks(i):
    def block(*parts):
        m = np.concatenate(parts, 1)
        k, n = m.shape
        return m.reshape(KT, P, n).transpose(1, 0, 2).reshape(P, BLK)

    def tall(m):
        u = [m[j * P:(j + 1) * P, h * 512:(h + 1) * 512] for h in range(2) for j in range(2 * KT)]
        return [np.stack(u[j:j + KT], 1).reshape(P, BLK) for j in range(0, len(u), KT)]

    out = [block(i["w_mod_2"][l][:, 512 * q:512 * (q + 1)]) for l in range(2) for q in range(6)]
    w = i["e_w_in_2"][0]
    q0 = 4 * D
    out += [block(*[w[:, p * D + c * P:p * D + (c + 1) * P] for p in (0, 1, 2, 3)]) for c in range(KT)]
    out.append(block(w[:, q0 + D:q0 + D + 512]))
    g0 = q0 + D + 512
    out += [block(w[:, q0 + 256 * j:q0 + 256 * (j + 1)], w[:, g0 + 256 * j:g0 + 256 * (j + 1)]) for j in range(4)]
    out += tall(i["e_w_out_2"][0])
    w = i["o_w_in_2"][0]
    for h in range(ML_HEADS):
        wide = [w[:, a + 256 * h:a + 256 * (h + 1)] for a in (2 * D, 4 * D, 6 * D)]
        out.append(block(w[:, P * h:P * (h + 1)], w[:, D + P * h:D + P * (h + 1)], wide[0]))
        out.append(block(wide[1], wide[2]))
    out += tall(i["o_w_out_2"][0])
    return out


def second_columns(i):
    def col(v):
        return np.asarray(v).reshape(-1, P).T

    parts = [np.stack([col(i["c_2"][0]), col(i["c_ctx_2"])], 2).reshape(P, 16)]
    for name in ("b_mod_2", "g_pre_2", "g_post_2"):
        parts.append(np.repeat(np.concatenate([col(i[name][l]) for l in range(2)], 1), 2, 1))
    hy = [[i["e_conv_w_2"][0][j, p * D + c * P:p * D + (c + 1) * P] for p in range(3) for j in range(3)]
          + [i["e_conv_b_2"][0][p * D + c * P:p * D + (c + 1) * P] for p in range(3)]
          + [i["e_hy_bias_2"][0][c * P:(c + 1) * P]] for c in range(KT)]
    parts.append(np.stack([v for c in hy for v in c], 1))
    parts.append(np.stack([i["e_q_norm_2"][0], i["e_k_norm_2"][0]], 1))
    ml = []
    for h in range(ML_HEADS):
        for base in (0, D):
            s = slice(base + P * h, base + P * (h + 1))
            ml += [i["o_conv_w_2"][0][j, s] for j in range(3)] + [i["o_conv_b_2"][0][s]]
        ml += [i["o_head_norm_2"][0][256 * h + P * t:256 * h + P * (t + 1)] for t in range(2)]
    parts.append(np.stack(ml, 1))
    gb = np.zeros((P, 2), np.float32)
    for g in range(4):
        p0 = 32 * (g // 2)
        gb[p0:p0 + ML_HEADS, g % 2] = i["o_gate_b_2"][0][ML_HEADS * g:ML_HEADS * (g + 1)]
    parts.append(gb)
    return np.concatenate(parts, 1)


def gate_weights(i):
    w = np.zeros((D, 2, 64), np.float32)
    for g in range(4):
        c0 = 32 * (g // 2)
        w[:, g % 2, c0:c0 + ML_HEADS] = i["o_w_in_2"][0][:, 8 * D + ML_HEADS * g:8 * D + ML_HEADS * (g + 1)]
    return np.ascontiguousarray(w.reshape(KT, P, 2, 64).transpose(1, 2, 0, 3).reshape(P, -1))


def filter_weights(i):
    f32 = np.float32
    t = np.linspace(0.0, 1.0, SEQ, dtype=f32)[:, None]
    bands = np.linspace(1e-4, (HY_EMB - 1) // 2 - 1, (HY_EMB - 1) // 2, dtype=f32)
    ang = f32(2.0 * np.pi / SEQ) * np.arange(SEQ, dtype=f32)[:, None] * bands
    feat = np.concatenate([t, np.cos(ang), -np.sin(ang)], -1).astype(f32)
    out = np.zeros((HY_HIDDEN, FILTCOLS), f32)
    out[:HY_EMB, :SEQ] = feat.T
    out[:HY_EMB, SEQ:SEQ + HY_HIDDEN] = i["e_filt_w1_2"][0]
    out[:, SEQ + HY_HIDDEN:SEQ + 2 * HY_HIDDEN] = i["e_filt_w2_2"][0]
    out[:, SEQ + 2 * HY_HIDDEN:FILTCOLS - 4] = i["e_filt_w3_2"][0]
    for j, name in enumerate(("e_filt_b1_2", "e_filt_b2_2", "e_filt_freq_2")):
        out[:, FILTCOLS - 4 + j] = i[name][0]
    return out


def resident_constants():
    f32 = np.float32
    turn = np.zeros((P, P), f32)
    for m in range(P):
        if m % 64 < 32:
            turn[m + 32, m] = -1.0
        else:
            turn[m - 32, m] = 1.0
    s, t = np.arange(P)[:, None], np.arange(P)[None, :]
    masks = [np.where(s > t, MASKED, 0.0), np.where(s < t, MASKED, 0.0)]
    inv = (f32(ROPE_THETA) ** (-np.arange(32, dtype=f32) / f32(32))).astype(f32)
    pos = np.arange(SEQ)
    rows_, cols_ = (pos // GRID_W).astype(f32), (pos % GRID_W).astype(f32)
    ang = np.concatenate([np.tile(inv[:, None] * p_[None, :], (2, 1)) for p_ in (rows_, cols_)], 0).astype(f32)
    return np.concatenate([np.eye(P), np.ones((P, P)), turn, *masks, np.cos(ang), np.sin(ang)], 1).astype(f32)


def hyena_constants():
    n2 = 2 * SEQ
    t, k = np.arange(SEQ)[:, None], np.arange(SEQ)[None, :]
    ang = 2 * np.pi * ((t * k) % n2) / n2
    alt = (-1.0) ** np.arange(SEQ)
    fwd_c, fwd_s = np.cos(ang), -np.sin(ang)
    nyq = fwd_c[:, :P].copy()
    nyq[:, 0] = alt
    both = fwd_s.copy()
    weight = np.where(np.arange(SEQ) == 0, 1.0, 2.0)[:, None] / n2
    inv_c, inv_s = weight * np.cos(ang.T), -weight * np.sin(ang.T)
    inv_s[0] = alt / n2

    def tiles(m):
        return m.reshape(-1, P, m.shape[1]).transpose(1, 0, 2).reshape(P, -1)

    tt = np.linspace(0.0, 1.0, SEQ, dtype=np.float32)[:, None]
    deltas = np.linspace(np.log(HY_TARGET) / HY_LONG_DECAY, np.log(HY_TARGET) / HY_SHORT_DECAY, D, dtype=np.float32)
    window = np.exp(-tt * np.abs(deltas))
    sgn = both.copy()
    sgn[:, 0] = alt
    return np.concatenate([tiles(fwd_c), tiles(sgn), tiles(inv_c), tiles(inv_s), tiles(nyq), tiles(window)], 1)\
        .astype(np.float32)


def columns(i):
    def col(m):
        return m.reshape(-1, P).T
    return np.concatenate([col(np.asarray(i[name][l]).reshape(-1)) for l in range(DEPTH) for name in LCOL], 1)


def kernel(**inputs):
    import concourse.bacc as bacc
    from concourse.bass_utils import run_bass_kernel_spmd

    i = {k: np.asarray(v) for k, v in inputs.items()}
    arrays = {
        "weights": np.stack(weight_blocks(i) + second_blocks(i)),
        "cols": np.ascontiguousarray(columns(i)),
        "lnrows": np.ascontiguousarray(np.stack([i["ln_g"], i["ln_b"]], 2).reshape(DEPTH * 6, D)),
        "consts": resident_constants(),
        "cols2": second_columns(i),
        "hy_consts": hyena_constants(),
        "filt": filter_weights(i),
        "gate_w": gate_weights(i),
        "ctx_rows": i["ctx_2"],
        "x": i["x"],
    }
    nc = bacc.Bacc("TRN2", target_bir_lowering=False, num_devices=1)
    args = {n: nc.dram_tensor(n, a.shape, mybir.dt.from_np(a.dtype), kind="ExternalInput").ap()
            for n, a in arrays.items()}
    out = nc.dram_tensor("out", (1, SEQ, D), F32, kind="ExternalOutput").ap()
    build(nc, out=out, **args)
    r = run_bass_kernel_spmd(nc, [arrays], core_ids=[0])
    return r.results[0]["out"]
```
